# Optimizing a Trainium2 kernel written in Bass

```python
import math
import jax, jax.numpy as jnp
from jax import lax
import numpy as np

D_MODEL = 1024
BATCH = 1
SEQ = 256
DEPTH = 1

MEM_LEN = 256
EPS = 1e-6

SSD_HEADS = 16
SSD_HEAD_DIM = 64
SSD_WIDTH = SSD_HEADS * SSD_HEAD_DIM
SSD_GROUPS = 4
SSD_STATE = 128
CONV_WIDTH = 4
SSD_CHUNK = 128
CONV_CH = SSD_WIDTH + 2 * SSD_GROUPS * SSD_STATE

DA_HEADS = 8
DA_HEAD_DIM = 64
DA_V_DIM = 2 * DA_HEAD_DIM
DA_WIDTH = DA_HEADS * DA_V_DIM
Q_BLOCK = 128

NUM_BUCKETS = 32
MAX_DISTANCE = 128

IN_SIZES = (SSD_WIDTH, CONV_CH, SSD_HEADS, DA_WIDTH, DA_WIDTH, DA_WIDTH)
IN_WIDTH = SSD_WIDTH + CONV_CH + SSD_HEADS + 3 * DA_WIDTH
MIX_WIDTH = SSD_WIDTH + DA_WIDTH

CROSS_HEADS = 4
CROSS_HEAD_DIM = D_MODEL // CROSS_HEADS

D_FF = 2816


def rms_norm(x, w):
    x32 = x.astype(jnp.float32)
    y = x32 * lax.rsqrt(jnp.mean(x32 * x32, axis=-1, keepdims=True) + EPS)
    return y.astype(x.dtype) * w

def swiglu(h, w_in, w_out):
    gate, up = jnp.split(h @ w_in, 2, axis=-1)
    return (jax.nn.silu(gate) * up) @ w_out

def split_sizes(u, sizes):
    idx, acc = [], 0
    for s in sizes[:-1]:
        acc += s
        idx.append(acc)
    return jnp.split(u, idx, axis=-1)

def causal_dwconv(u, w, b):
    y = lax.conv_general_dilated(u, w[:, None, :], window_strides=(1,),
                                 padding=[(CONV_WIDTH - 1, 0)],
                                 dimension_numbers=('NWC', 'WIO', 'NWC'),
                                 feature_group_count=u.shape[-1])
    return y + b

def ssd_scan(xh, dt, a, b_in, c_in):
    bsz, seqlen, nh, hp = xh.shape
    ng, ns = b_in.shape[2], b_in.shape[3]
    r = nh // ng
    nc = seqlen // SSD_CHUNK
    xdt = (xh * dt[..., None]).reshape(bsz, nc, SSD_CHUNK, ng, r, hp)
    la = (dt * a).reshape(bsz, nc, SSD_CHUNK, ng, r)
    bc = b_in.reshape(bsz, nc, SSD_CHUNK, ng, ns)
    cc = c_in.reshape(bsz, nc, SSD_CHUNK, ng, ns)
    la_cum = jnp.cumsum(la, axis=2)
    causal = jnp.tril(jnp.ones((SSD_CHUNK, SSD_CHUNK), dtype=bool))
    seg = la_cum[:, :, :, None] - la_cum[:, :, None, :]
    decay = jnp.exp(jnp.where(causal[None, None, :, :, None, None], seg, -jnp.inf))
    cb = jnp.einsum('bclgn,bcsgn->bclsg', cc, bc)
    y_diag = jnp.einsum('bclsg,bclsgr,bcsgrp->bclgrp', cb, decay, xdt)
    decay_to_end = jnp.exp(la_cum[:, :, -1:] - la_cum)
    chunk_states = jnp.einsum('bclgn,bclgr,bclgrp->bcgrpn', bc, decay_to_end, xdt)
    chunk_decay = jnp.exp(la_cum[:, :, -1])

    def step(state, inp):
        st, dec = inp
        return state * dec[..., None, None] + st, state

    init = jnp.zeros_like(chunk_states[:, 0])
    _, prev = lax.scan(step, init, (jnp.moveaxis(chunk_states, 1, 0),
                                    jnp.moveaxis(chunk_decay, 1, 0)))
    prev = jnp.moveaxis(prev, 0, 1)
    y_off = jnp.einsum('bclgn,bcgrpn,bclgr->bclgrp', cc, prev, jnp.exp(la_cum))
    return (y_diag + y_off).reshape(bsz, seqlen, nh, hp)

def rel_bucket(rel):
    n = jnp.maximum(-rel, 0)
    max_exact = NUM_BUCKETS // 2
    nf = jnp.maximum(n, 1).astype(jnp.float32)
    large = max_exact + (jnp.log(nf / max_exact) / math.log(MAX_DISTANCE / max_exact)
                         * (NUM_BUCKETS - max_exact)).astype(jnp.int32)
    large = jnp.minimum(large, NUM_BUCKETS - 1)
    return jnp.where(n < max_exact, n, large)

def diff_attention(q, k, v, lam, rel_bias):
    bsz, seqlen, nh, _, dh = q.shape
    nb = seqlen // Q_BLOCK
    scale = dh ** -0.5
    qb = jnp.moveaxis(q.reshape(bsz, nb, Q_BLOCK, nh, 2, dh), 1, 0)
    k_pos = jnp.arange(seqlen)

    def block(args):
        q_blk, i = args
        q_pos = i * Q_BLOCK + jnp.arange(Q_BLOCK)
        rel = k_pos[None, :] - q_pos[:, None]
        bias = jnp.transpose(rel_bias[rel_bucket(rel)], (2, 0, 1)).astype(jnp.float32)
        logits = jnp.einsum('bqhcd,bkhcd->bhcqk', q_blk, k,
                            preferred_element_type=jnp.float32) * scale
        logits = logits + bias[None, :, None]
        logits = jnp.where(rel[None, None, None] <= 0, logits, -jnp.inf)
        p = jax.nn.softmax(logits, axis=-1)
        w = p[:, :, 0] - lam * p[:, :, 1]
        return jnp.einsum('bhqk,bkhe->bqhe', w.astype(v.dtype), v,
                          preferred_element_type=jnp.float32)

    out = lax.map(block, (qb, jnp.arange(nb)))
    return jnp.moveaxis(out, 0, 1).reshape(bsz, seqlen, nh, 2 * dh)

def hybrid_mixer(h, w_in, conv_w, conv_b, dt_bias, a_log, d_skip, ssd_norm_w,
                 lq1, lk1, lq2, lk2, subln_w, rel_bias, w_out, lambda_init):
    bsz, seqlen, _ = h.shape
    z, xbc, dt_raw, q, k, v = split_sizes(h @ w_in, IN_SIZES)

    xbc = jax.nn.silu(causal_dwconv(xbc, conv_w, conv_b))
    xs, bs, cs = jnp.split(xbc, [SSD_WIDTH, SSD_WIDTH + SSD_GROUPS * SSD_STATE], axis=-1)
    dt = jax.nn.softplus(dt_raw.astype(jnp.float32) + dt_bias.astype(jnp.float32))
    a = -jnp.exp(a_log.astype(jnp.float32))
    xh = xs.reshape(bsz, seqlen, SSD_HEADS, SSD_HEAD_DIM).astype(jnp.float32)
    y = ssd_scan(xh, dt, a,
                 bs.reshape(bsz, seqlen, SSD_GROUPS, SSD_STATE).astype(jnp.float32),
                 cs.reshape(bsz, seqlen, SSD_GROUPS, SSD_STATE).astype(jnp.float32))
    y = y + d_skip.astype(jnp.float32)[:, None] * xh
    y = y.reshape(bsz, seqlen, SSD_WIDTH) * jax.nn.silu(z.astype(jnp.float32))
    yg = y.reshape(bsz, seqlen, SSD_GROUPS, SSD_WIDTH // SSD_GROUPS)
    yg = yg * lax.rsqrt(jnp.mean(yg * yg, axis=-1, keepdims=True) + EPS)
    y_ssd = yg.reshape(bsz, seqlen, SSD_WIDTH).astype(h.dtype) * ssd_norm_w

    q = q.reshape(bsz, seqlen, DA_HEADS, 2, DA_HEAD_DIM)
    k = k.reshape(bsz, seqlen, DA_HEADS, 2, DA_HEAD_DIM)
    v = v.reshape(bsz, seqlen, DA_HEADS, DA_V_DIM)
    lam = (jnp.exp(jnp.sum(lq1.astype(jnp.float32) * lk1.astype(jnp.float32)))
           - jnp.exp(jnp.sum(lq2.astype(jnp.float32) * lk2.astype(jnp.float32)))
           + lambda_init)
    o = diff_attention(q, k, v, lam, rel_bias)
    o = o * lax.rsqrt(jnp.mean(o * o, axis=-1, keepdims=True) + EPS)
    y_attn = (o.astype(h.dtype) * subln_w * (1.0 - lambda_init)).reshape(bsz, seqlen, DA_WIDTH)

    return jnp.concatenate([y_ssd, y_attn], axis=-1) @ w_out

def memory_cross_attention(h, mem_n, w_cq, w_ck, w_cv, w_co):
    bsz, seqlen, _ = h.shape
    mlen = mem_n.shape[1]
    q = (h @ w_cq).reshape(bsz, seqlen, CROSS_HEADS, CROSS_HEAD_DIM)
    k = (mem_n @ w_ck).reshape(bsz, mlen, CROSS_HEADS, CROSS_HEAD_DIM)
    v = (mem_n @ w_cv).reshape(bsz, mlen, CROSS_HEADS, CROSS_HEAD_DIM)
    logits = jnp.einsum('bqhd,bkhd->bhqk', q, k,
                        preferred_element_type=jnp.float32) * (CROSS_HEAD_DIM ** -0.5)
    p = jax.nn.softmax(logits, axis=-1)
    o = jnp.einsum('bhqk,bkhd->bqhd', p.astype(v.dtype), v).reshape(bsz, seqlen, D_MODEL)
    return o @ w_co

def first_inputs(seed: int = 0) -> dict:
    key = jax.random.key(seed)
    ks = jax.random.split(key, 32)
    f32 = jnp.float32

    def nrm(k, shape, scale):
        return jax.random.normal(k, shape, f32) * scale

    def gain(k, shape):
        return 1.0 + 0.02 * jax.random.normal(k, shape, f32)

    L = DEPTH
    dt0 = jnp.exp(jax.random.uniform(ks[10], (L, SSD_HEADS), f32,
                                     math.log(1e-3), math.log(1e-1)))
    dt_bias = dt0 + jnp.log(-jnp.expm1(-dt0))
    a_log = jnp.log(jax.random.uniform(ks[11], (L, SSD_HEADS), f32, 1.0, 16.0))
    return {
        'x': jax.random.normal(ks[0], (BATCH, SEQ, D_MODEL), f32),
        'mem': jax.random.normal(ks[1], (BATCH, MEM_LEN, D_MODEL), f32),
        'norm_ffn1_w': gain(ks[2], (L, D_MODEL)),
        'ffn1_w_in': nrm(ks[3], (L, D_MODEL, 2 * D_FF), D_MODEL ** -0.5),
        'ffn1_w_out': nrm(ks[4], (L, D_FF, D_MODEL), D_FF ** -0.5),
        'norm_mix_w': gain(ks[5], (L, D_MODEL)),
        'w_in_mix': nrm(ks[6], (L, D_MODEL, IN_WIDTH), D_MODEL ** -0.5),
        'conv_w': nrm(ks[7], (L, CONV_WIDTH, CONV_CH), CONV_WIDTH ** -0.5),
        'conv_b': nrm(ks[8], (L, CONV_CH), 0.01),
        'dt_bias': dt_bias,
        'a_log': a_log,
        'd_skip': gain(ks[9], (L, SSD_HEADS)),
        'ssd_norm_w': gain(ks[12], (L, SSD_WIDTH)),
        'lambda_q1': nrm(ks[13], (L, DA_HEAD_DIM), 0.1),
        'lambda_k1': nrm(ks[14], (L, DA_HEAD_DIM), 0.1),
        'lambda_q2': nrm(ks[15], (L, DA_HEAD_DIM), 0.1),
        'lambda_k2': nrm(ks[16], (L, DA_HEAD_DIM), 0.1),
        'subln_w': gain(ks[17], (L, DA_V_DIM)),
        'rel_bias': nrm(ks[18], (NUM_BUCKETS, DA_HEADS), 0.2),
        'w_out_mix': nrm(ks[19], (L, MIX_WIDTH, D_MODEL), MIX_WIDTH ** -0.5),
        'norm_cross_w': gain(ks[20], (L, D_MODEL)),
        'norm_mem_w': gain(ks[21], (L, D_MODEL)),
        'w_cq': nrm(ks[22], (L, D_MODEL, D_MODEL), D_MODEL ** -0.5),
        'w_ck': nrm(ks[23], (L, D_MODEL, D_MODEL), D_MODEL ** -0.5),
        'w_cv': nrm(ks[24], (L, D_MODEL, D_MODEL), D_MODEL ** -0.5),
        'w_co': nrm(ks[25], (L, D_MODEL, D_MODEL), D_MODEL ** -0.5),
        'norm_ffn2_w': gain(ks[26], (L, D_MODEL)),
        'ffn2_w_in': nrm(ks[27], (L, D_MODEL, 2 * D_FF), D_MODEL ** -0.5),
        'ffn2_w_out': nrm(ks[28], (L, D_FF, D_MODEL), D_FF ** -0.5),
        'norm_final_w': gain(ks[29], (D_MODEL,)),
    }

def first_block(x, mem, norm_ffn1_w, ffn1_w_in, ffn1_w_out, norm_mix_w, w_in_mix,
              conv_w, conv_b, dt_bias, a_log, d_skip, ssd_norm_w,
              lambda_q1, lambda_k1, lambda_q2, lambda_k2, subln_w, rel_bias,
              w_out_mix, norm_cross_w, norm_mem_w, w_cq, w_ck, w_cv, w_co,
              norm_ffn2_w, ffn2_w_in, ffn2_w_out, norm_final_w):
    for l in range(DEPTH):
        lambda_init = 0.8 - 0.6 * math.exp(-0.3 * l)
        x = x + 0.5 * swiglu(rms_norm(x, norm_ffn1_w[l]), ffn1_w_in[l], ffn1_w_out[l])
        x = x + hybrid_mixer(rms_norm(x, norm_mix_w[l]), w_in_mix[l], conv_w[l], conv_b[l],
                             dt_bias[l], a_log[l], d_skip[l], ssd_norm_w[l],
                             lambda_q1[l], lambda_k1[l], lambda_q2[l], lambda_k2[l],
                             subln_w[l], rel_bias, w_out_mix[l], lambda_init)
        x = x + memory_cross_attention(rms_norm(x, norm_cross_w[l]),
                                       rms_norm(mem, norm_mem_w[l]),
                                       w_cq[l], w_ck[l], w_cv[l], w_co[l])
        x = x + 0.5 * swiglu(rms_norm(x, norm_ffn2_w[l]), ffn2_w_in[l], ffn2_w_out[l])
    return rms_norm(x, norm_final_w)


DEPTH_2 = 2

N_MIXERS = 4
N_MEM = 256
NEG = -1e30
D_FF_2 = ((8 * D_MODEL // 3 + 255) // 256) * 256

POOL_WINDOWS = (2, 4, 8, 16)
POOL_GROUP = D_MODEL // len(POOL_WINDOWS)

NSA_HEADS = 16
NSA_KV_HEADS = 4
NSA_HEAD_DIM = D_MODEL // NSA_HEADS
NSA_CMP_BLOCK = 32
NSA_CMP_STRIDE = 16
NSA_SEL_BLOCK = 64
NSA_N_SELECT = 16
NSA_WINDOW = 512
NSA_CMP_HIDDEN = 4 * NSA_HEAD_DIM
NSA_Q_BLOCK = 64
NSA_KV_WIDTH = NSA_KV_HEADS * NSA_HEAD_DIM
NSA_FORCE = 1e4
NSA_IN_WIDTH = D_MODEL + 6 * NSA_KV_WIDTH + 3 * NSA_HEADS

GLA_HEADS = 4
GLA_DK = D_MODEL // 2 // GLA_HEADS
GLA_DV = D_MODEL // GLA_HEADS
GLA_GATE_RANK = 16
GLA_TAU = 16.0
GLA_CHUNK = 64
GLA_IN_WIDTH = 2 * GLA_HEADS * GLA_DK + 2 * GLA_HEADS * GLA_DV + GLA_GATE_RANK

CONV_WIDTH_2 = 31

XATTN_HEADS = 4
XATTN_HEAD_DIM = D_MODEL // XATTN_HEADS


F32 = jnp.float32

def n_layers_of(m):
    return len(range(m, DEPTH_2, N_MIXERS))

def rms_norm_2(x, g):
    xf = x.astype(F32)
    y = xf * lax.rsqrt(jnp.mean(xf * xf, axis=-1, keepdims=True) + EPS)
    return (y * g.astype(F32)).astype(x.dtype)

def swiglu_ffn(h, w_in, w_out):
    g, u = jnp.split(h @ w_in, 2, axis=-1)
    return (jax.nn.silu(g) * u) @ w_out

def pool_mixer(h, w, b, scale):
    B, S, D = h.shape
    hf = h.astype(F32)
    c = jnp.pad(jnp.cumsum(hf, axis=1), ((0, 0), (1, 0), (0, 0)))
    t = jnp.arange(S)
    groups = []
    for gi, win in enumerate(POOL_WINDOWS):
        cg = c[:, :, gi * POOL_GROUP:(gi + 1) * POOL_GROUP]
        start = jnp.maximum(t + 1 - win, 0)
        win_sum = cg[:, 1:] - jnp.take(cg, start, axis=1)
        cnt = (t + 1 - start).astype(F32)[None, :, None]
        groups.append(win_sum / cnt - hf[:, :, gi * POOL_GROUP:(gi + 1) * POOL_GROUP])
    p = jnp.stack(groups, axis=2)
    y = jnp.einsum('bsgc,gcd->bsgd', p, w.astype(F32)).reshape(B, S, D) + b.astype(F32)
    return (y * scale.astype(F32)).astype(h.dtype)

def nsa_mixer(h, w_in, cmp_pos, cmp_w1, cmp_w2, w_o):
    B, S, D = h.shape
    H, G, dh = NSA_HEADS, NSA_KV_HEADS, NSA_HEAD_DIM
    R = H // G
    SEL = NSA_SEL_BLOCK
    proj = (h @ w_in).astype(F32)
    splits = np.cumsum([D] + [NSA_KV_WIDTH] * 6).tolist()
    q, kc, vc, ks, vs, kw, vw, gates = jnp.split(proj, splits, axis=-1)
    q = q.reshape(B, S, G, R, dh).transpose(0, 2, 3, 1, 4) * dh ** -0.5
    gates = jax.nn.sigmoid(gates).reshape(B, S, G, R, 3).transpose(0, 2, 3, 1, 4)

    def kv_heads(a):
        return a.reshape(B, S, G, dh).transpose(0, 2, 1, 3)

    n_cmp = (S - NSA_CMP_BLOCK) // NSA_CMP_STRIDE + 1
    cmp_idx = np.arange(n_cmp)[:, None] * NSA_CMP_STRIDE + np.arange(NSA_CMP_BLOCK)[None, :]

    def compress(a, pos, w1, w2):
        blk = (a[:, :, cmp_idx] + pos.astype(F32)).reshape(B, G, n_cmp, NSA_CMP_BLOCK * dh)
        return jax.nn.gelu(blk @ w1.astype(F32)) @ w2.astype(F32)

    k_cmp = compress(kv_heads(kc), cmp_pos[0], cmp_w1[0], cmp_w2[0])
    v_cmp = compress(kv_heads(vc), cmp_pos[1], cmp_w1[1], cmp_w2[1])
    cmp_end = jnp.asarray(cmp_idx[:, -1])

    n_slc = S // SEL
    cs = np.arange(n_cmp) * NSA_CMP_STRIDE
    ss = np.arange(n_slc) * SEL
    ov = np.clip(np.minimum(cs[:, None] + NSA_CMP_BLOCK, ss[None, :] + SEL)
                 - np.maximum(cs[:, None], ss[None, :]), 0, None) / NSA_CMP_BLOCK
    ov = jnp.asarray(ov, F32)
    k_eff = min(NSA_N_SELECT, n_slc)
    blk_ids = jnp.arange(n_slc)

    ks_blk = kv_heads(ks).reshape(B, G, n_slc, SEL, dh)
    vs_blk = kv_heads(vs).reshape(B, G, n_slc, SEL, dh)
    kw_pad = jnp.pad(kv_heads(kw), ((0, 0), (0, 0), (NSA_WINDOW, 0), (0, 0)))
    vw_pad = jnp.pad(kv_heads(vw), ((0, 0), (0, 0), (NSA_WINDOW, 0), (0, 0)))
    bi = jnp.arange(B)[:, None, None, None]
    gi = jnp.arange(G)[None, :, None, None]
    Qb = min(NSA_Q_BLOCK, S)
    n_qb = S // Qb

    def block(qi):
        s0 = qi * Qb
        t = s0 + jnp.arange(Qb)
        qb = lax.dynamic_slice_in_dim(q, s0, Qb, axis=3)
        gb = lax.dynamic_slice_in_dim(gates, s0, Qb, axis=3)
        vis = cmp_end[None, :] <= t[:, None]
        sc = jnp.where(vis, jnp.einsum('bgrqd,bgnd->bgrqn', qb, k_cmp), NEG)
        p_cmp = jax.nn.softmax(sc, axis=-1) * jnp.any(vis, axis=-1)[:, None]
        o_cmp = jnp.einsum('bgrqn,bgnd->bgrqd', p_cmp, v_cmp)
        imp = jnp.einsum('bgrqn,nm->bgqm', p_cmp, ov)
        cur = t // SEL
        forced = (blk_ids[None, :] == 0) | (blk_ids[None, :] == cur[:, None]) | (blk_ids[None, :] == cur[:, None] - 1)
        imp = jnp.where(forced, NSA_FORCE, imp)
        imp = jnp.where(blk_ids[None, :] * SEL <= t[:, None], imp, -1.0)
        _, idx = lax.top_k(imp, k_eff)
        ksel = ks_blk[bi, gi, idx].reshape(B, G, Qb, k_eff * SEL, dh)
        vsel = vs_blk[bi, gi, idx].reshape(B, G, Qb, k_eff * SEL, dh)
        pos = (idx[..., None] * SEL + jnp.arange(SEL)).reshape(B, G, Qb, k_eff * SEL)
        sc = jnp.einsum('bgrqd,bgqkd->bgrqk', qb, ksel)
        sc = jnp.where((pos <= t[:, None])[:, :, None], sc, NEG)
        o_slc = jnp.einsum('bgrqk,bgqkd->bgrqd', jax.nn.softmax(sc, axis=-1), vsel)
        kwin = lax.dynamic_slice_in_dim(kw_pad, s0, NSA_WINDOW + Qb, axis=2)
        vwin = lax.dynamic_slice_in_dim(vw_pad, s0, NSA_WINDOW + Qb, axis=2)
        wpos = s0 - NSA_WINDOW + jnp.arange(NSA_WINDOW + Qb)
        wmask = (wpos[None, :] <= t[:, None]) & (wpos[None, :] > t[:, None] - NSA_WINDOW) & (wpos[None, :] >= 0)
        sc = jnp.where(wmask, jnp.einsum('bgrqd,bgkd->bgrqk', qb, kwin), NEG)
        o_win = jnp.einsum('bgrqk,bgkd->bgrqd', jax.nn.softmax(sc, axis=-1), vwin)
        return gb[..., 0:1] * o_cmp + gb[..., 1:2] * o_slc + gb[..., 2:3] * o_win

    o = lax.map(block, jnp.arange(n_qb))
    o = o.transpose(1, 0, 4, 2, 3, 5).reshape(B, S, H * dh)
    return o.astype(h.dtype) @ w_o

def gla_mixer(h, w_in, w_gate_up, b_gate, norm_g, w_o):
    B, S, D = h.shape
    Hh, dk, dv, C = GLA_HEADS, GLA_DK, GLA_DV, GLA_CHUNK
    proj = (h @ w_in).astype(F32)
    qw, vw = Hh * dk, Hh * dv
    q, k, v, og, gdown = jnp.split(proj, [qw, 2 * qw, 2 * qw + vw, 2 * qw + 2 * vw], axis=-1)
    log_a = jax.nn.log_sigmoid(gdown @ w_gate_up.astype(F32) + b_gate.astype(F32)) / GLA_TAU
    nc = S // C

    def heads(a, d):
        return a.reshape(B, nc, C, Hh, d).transpose(0, 3, 1, 2, 4)

    q = heads(q, dk) * dk ** -0.5
    k = heads(k, dk)
    v = heads(v, dv)
    b = jnp.cumsum(heads(log_a, dk), axis=3)
    b_last = b[:, :, :, -1:, :]
    q_t = q * jnp.exp(b)
    k_t = k * jnp.exp(-b)
    causal = jnp.tril(jnp.ones((C, C), dtype=bool))
    A = jnp.where(causal, jnp.einsum('bhncd,bhnsd->bhncs', q_t, k_t), 0.0)
    o_intra = jnp.einsum('bhncs,bhnsv->bhncv', A, v)
    kv = jnp.einsum('bhncd,bhncv->bhndv', k * jnp.exp(b_last - b), v)
    decay = jnp.exp(b_last[:, :, :, 0, :])

    def step(state, inp):
        kv_n, dec_n = inp
        return dec_n[..., None] * state + kv_n, state

    init = jnp.zeros((B, Hh, dk, dv), F32)
    _, s_prev = lax.scan(step, init, (kv.transpose(2, 0, 1, 3, 4), decay.transpose(2, 0, 1, 3)))
    s_prev = s_prev.transpose(1, 2, 0, 3, 4)
    o = o_intra + jnp.einsum('bhncd,bhndv->bhncv', q_t, s_prev)
    o = rms_norm_2(o.transpose(0, 2, 3, 1, 4).reshape(B, S, Hh, dv), norm_g)
    o = o.reshape(B, S, Hh * dv) * jax.nn.silu(og)
    return o.astype(h.dtype) @ w_o

def conv_mixer(h, w_in, b_in, w_dw, b_dw, ln_g, ln_b, w_out, b_out):
    D = h.shape[-1]
    a, gate = jnp.split(h @ w_in + b_in, 2, axis=-1)
    u = a * jax.nn.sigmoid(gate)
    u = jnp.pad(u, ((0, 0), (CONV_WIDTH_2 - 1, 0), (0, 0)))
    u = lax.conv_general_dilated(u, w_dw[:, None, :].astype(u.dtype), window_strides=(1,), padding='VALID',
                                 dimension_numbers=('NWC', 'WIO', 'NWC'), feature_group_count=D) + b_dw
    uf = u.astype(F32)
    mu = jnp.mean(uf, axis=-1, keepdims=True)
    var = jnp.mean(jnp.square(uf - mu), axis=-1, keepdims=True)
    uf = (uf - mu) * lax.rsqrt(var + EPS) * ln_g.astype(F32) + ln_b.astype(F32)
    return jax.nn.silu(uf).astype(h.dtype) @ w_out + b_out

def memory_cross_attention_2(h, mem_n, w_q, w_kv, w_o):
    B, S, D = h.shape
    N = mem_n.shape[1]
    Hx, dh = XATTN_HEADS, XATTN_HEAD_DIM
    q = (h @ w_q).astype(F32).reshape(B, S, Hx, dh) * dh ** -0.5
    k, v = jnp.split((mem_n @ w_kv).astype(F32), 2, axis=-1)
    k = k.reshape(B, N, Hx, dh)
    v = v.reshape(B, N, Hx, dh)
    p = jax.nn.softmax(jnp.einsum('bqhd,bkhd->bhqk', q, k), axis=-1)
    o = jnp.einsum('bhqk,bkhd->bqhd', p, v).reshape(B, S, D)
    return o.astype(h.dtype) @ w_o

def second_inputs(seed: int = 0) -> dict:
    key = jax.random.key(seed)
    keys = iter(jax.random.split(key, 64))
    D, F, L = D_MODEL, D_FF_2, DEPTH_2
    nA, nB, nC, nD = (n_layers_of(m) for m in range(N_MIXERS))

    def w(shape, fan_in):
        return jax.random.normal(next(keys), shape, F32) * fan_in ** -0.5

    def gain(shape):
        return 1.0 + 0.02 * jax.random.normal(next(keys), shape, F32)

    def small(shape, s=0.02):
        return s * jax.random.normal(next(keys), shape, F32)

    return {
        "x": jax.random.normal(next(keys), (BATCH, SEQ, D), F32),
        "mem": jax.random.normal(next(keys), (BATCH, N_MEM, D), F32),
        "ffn1_norm": gain((L, D)),
        "ffn1_w_in": w((L, D, 2 * F), D),
        "ffn1_w_out": w((L, F, D), F),
        "mix_norm": gain((L, D)),
        "xattn_norm": gain((L, D)),
        "mem_norm": gain((L, D)),
        "xattn_w_q": w((L, D, D), D),
        "xattn_w_kv": w((L, D, 2 * D), D),
        "xattn_w_o": w((L, D, D), D),
        "ffn2_norm": gain((L, D)),
        "ffn2_w_in": w((L, D, 2 * F), D),
        "ffn2_w_out": w((L, F, D), F),
        "pool_w": w((nA, len(POOL_WINDOWS), POOL_GROUP, POOL_GROUP), POOL_GROUP),
        "pool_b": small((nA, D)),
        "pool_scale": 1.0 + 0.1 * jax.random.normal(next(keys), (nA, D), F32),
        "nsa_w_in": w((nB, D, NSA_IN_WIDTH), D),
        "nsa_cmp_pos": small((nB, 2, NSA_CMP_BLOCK, NSA_HEAD_DIM), 0.1),
        "nsa_cmp_w1": w((nB, 2, NSA_CMP_BLOCK * NSA_HEAD_DIM, NSA_CMP_HIDDEN), NSA_CMP_BLOCK * NSA_HEAD_DIM),
        "nsa_cmp_w2": w((nB, 2, NSA_CMP_HIDDEN, NSA_HEAD_DIM), NSA_CMP_HIDDEN),
        "nsa_w_o": w((nB, D, D), D),
        "gla_w_in": w((nC, D, GLA_IN_WIDTH), D),
        "gla_w_gate_up": w((nC, GLA_GATE_RANK, GLA_HEADS * GLA_DK), GLA_GATE_RANK),
        "gla_b_gate": small((nC, GLA_HEADS * GLA_DK)),
        "gla_norm": gain((nC, GLA_DV)),
        "gla_w_o": w((nC, D, D), D),
        "conv_w_in": w((nD, D, 2 * D), D),
        "conv_b_in": small((nD, 2 * D)),
        "conv_dw": w((nD, CONV_WIDTH_2, D), CONV_WIDTH_2),
        "conv_b_dw": small((nD, D)),
        "conv_ln_g": gain((nD, D)),
        "conv_ln_b": small((nD, D)),
        "conv_w_out": w((nD, D, D), D),
        "conv_b_out": small((nD, D)),
        "final_norm": gain((D,)),
    }

def second_block(x, mem, ffn1_norm, ffn1_w_in, ffn1_w_out, mix_norm, xattn_norm, mem_norm,
              xattn_w_q, xattn_w_kv, xattn_w_o, ffn2_norm, ffn2_w_in, ffn2_w_out,
              pool_w, pool_b, pool_scale,
              nsa_w_in, nsa_cmp_pos, nsa_cmp_w1, nsa_cmp_w2, nsa_w_o,
              gla_w_in, gla_w_gate_up, gla_b_gate, gla_norm, gla_w_o,
              conv_w_in, conv_b_in, conv_dw, conv_b_dw, conv_ln_g, conv_ln_b, conv_w_out, conv_b_out,
              final_norm):
    for i in range(DEPTH_2):
        m, j = i % N_MIXERS, i // N_MIXERS
        x = x + 0.5 * swiglu_ffn(rms_norm_2(x, ffn1_norm[i]), ffn1_w_in[i], ffn1_w_out[i])
        h = rms_norm_2(x, mix_norm[i])
        if m == 0:
            y = pool_mixer(h, pool_w[j], pool_b[j], pool_scale[j])
        elif m == 1:
            y = nsa_mixer(h, nsa_w_in[j], nsa_cmp_pos[j], nsa_cmp_w1[j], nsa_cmp_w2[j], nsa_w_o[j])
        elif m == 2:
            y = gla_mixer(h, gla_w_in[j], gla_w_gate_up[j], gla_b_gate[j], gla_norm[j], gla_w_o[j])
        else:
            y = conv_mixer(h, conv_w_in[j], conv_b_in[j], conv_dw[j], conv_b_dw[j],
                           conv_ln_g[j], conv_ln_b[j], conv_w_out[j], conv_b_out[j])
        x = x + y
        x = x + memory_cross_attention_2(rms_norm_2(x, xattn_norm[i]), rms_norm_2(mem, mem_norm[i]),
                                       xattn_w_q[i], xattn_w_kv[i], xattn_w_o[i])
        x = x + 0.5 * swiglu_ffn(rms_norm_2(x, ffn2_norm[i]), ffn2_w_in[i], ffn2_w_out[i])
    return rms_norm_2(x, final_norm)


def setup_inputs(seed=0):
    out = dict(first_inputs(seed))
    for name, value in second_inputs(seed + 1).items():
        if name != "x":
            out[name + "_2"] = value
    return out


def reference(
    x, mem, norm_ffn1_w, ffn1_w_in, ffn1_w_out, norm_mix_w, w_in_mix, conv_w, conv_b, dt_bias,
    a_log, d_skip, ssd_norm_w, lambda_q1, lambda_k1, lambda_q2, lambda_k2, subln_w, rel_bias,
    w_out_mix, norm_cross_w, norm_mem_w, w_cq, w_ck, w_cv, w_co, norm_ffn2_w, ffn2_w_in,
    ffn2_w_out, norm_final_w, mem_2, ffn1_norm_2, ffn1_w_in_2, ffn1_w_out_2, mix_norm_2,
    xattn_norm_2, mem_norm_2, xattn_w_q_2, xattn_w_kv_2, xattn_w_o_2, ffn2_norm_2, ffn2_w_in_2,
    ffn2_w_out_2, pool_w_2, pool_b_2, pool_scale_2, nsa_w_in_2, nsa_cmp_pos_2, nsa_cmp_w1_2,
    nsa_cmp_w2_2, nsa_w_o_2, gla_w_in_2, gla_w_gate_up_2, gla_b_gate_2, gla_norm_2, gla_w_o_2,
    conv_w_in_2, conv_b_in_2, conv_dw_2, conv_b_dw_2, conv_ln_g_2, conv_ln_b_2, conv_w_out_2,
    conv_b_out_2, final_norm_2,
):
    x = first_block(
        x, mem, norm_ffn1_w, ffn1_w_in, ffn1_w_out, norm_mix_w, w_in_mix, conv_w, conv_b,
        dt_bias, a_log, d_skip, ssd_norm_w, lambda_q1, lambda_k1, lambda_q2, lambda_k2, subln_w,
        rel_bias, w_out_mix, norm_cross_w, norm_mem_w, w_cq, w_ck, w_cv, w_co, norm_ffn2_w,
        ffn2_w_in, ffn2_w_out, norm_final_w,
    )
    return second_block(
        x, mem_2, ffn1_norm_2, ffn1_w_in_2, ffn1_w_out_2, mix_norm_2, xattn_norm_2, mem_norm_2,
        xattn_w_q_2, xattn_w_kv_2, xattn_w_o_2, ffn2_norm_2, ffn2_w_in_2, ffn2_w_out_2,
        pool_w_2, pool_b_2, pool_scale_2, nsa_w_in_2, nsa_cmp_pos_2, nsa_cmp_w1_2, nsa_cmp_w2_2,
        nsa_w_o_2, gla_w_in_2, gla_w_gate_up_2, gla_b_gate_2, gla_norm_2, gla_w_o_2,
        conv_w_in_2, conv_b_in_2, conv_dw_2, conv_b_dw_2, conv_ln_g_2, conv_ln_b_2,
        conv_w_out_2, conv_b_out_2, final_norm_2,
    )


_drawn_inputs = setup_inputs


def setup_inputs(seed=0):
    import zlib

    import numpy as np

    out = dict(_drawn_inputs(seed))
    spreads = {}
    factors = {'norm_ffn1_w': 4.556,
     'conv_b': 6.933,
     'd_skip': 6.235,
     'ssd_norm_w': 4.716,
     'lambda_k1': 3.31,
     'lambda_k2': 2.981,
     'subln_w': 6.307,
     'norm_cross_w': 8.0,
     'norm_mem_w': 8.0,
     'norm_ffn2_w': 8.0,
     'ffn1_norm_2': 5.314,
     'mix_norm_2': 3.936,
     'xattn_norm_2': 8.0,
     'mem_norm_2': 8.0,
     'ffn2_norm_2': 6.51,
     'pool_b_2': 3.233,
     'nsa_cmp_pos_2': 2.759,
     'final_norm_2': 2.806}
    for name, (base, spread) in spreads.items():
        noise = np.random.default_rng([zlib.crc32(name.encode()), seed]).standard_normal(out[name].shape)
        drawn = base * np.exp(spread * noise) if base else spread * noise
        out[name] = __import__('jax').numpy.asarray(drawn.astype(out[name].dtype))
    for name, factor in factors.items():
        out[name] = (out[name] * factor).astype(out[name].dtype)
    return out
```

```python
from contextlib import ExitStack
import math

import numpy as np

import concourse.bass as bass
from concourse import mybir

F32 = mybir.dt.float32
F32R = mybir.dt.float32r
BF16 = mybir.dt.bfloat16
ALU = mybir.AluOpType
ACT = mybir.ActivationFunctionType
AX_X = mybir.AxisListType.X

P = 128
S = 256
D = 1024
TT = S // P
KC = D // P
F = 2816
FI = F // 256
EPS = 1e-6
NEG = -1e30

RAW = 3
SPL = 3

SSD_HEADS, SSD_P, SSD_GROUPS, CONV_W = 16, 64, 4, 4
DA_HEADS, DA_DIM = 8, 64
BUCKETS, MAX_DIST = 32, 128
X_HEADS, X_DIM = 4, 256
NSA_HEADS, NSA_KV, NSA_DIM = 16, 4, 64
CMP_BLOCK, CMP_STRIDE = 32, 16
NCMP = (S - CMP_BLOCK) // CMP_STRIDE + 1
WINDOWS = (2, 4, 8, 16)
LAMBDA_INIT = 0.8 - 0.6 * math.exp(0.0)

T_FFN, T_MIXIN, T_MIXOUT, T_XKV, T_XQO, T_POOL, T_NSAIN, T_NSAOUT = 33, 24, 8, 8, 8, 1, 14, 4

STAGES = ["ffn", "mixer", "cross", "ffn", "blocknorm",
          "ffn", "pool", "cross", "ffn",
          "ffn", "nsa", "cross", "ffn", "finalnorm"]
TILES = {"ffn": T_FFN, "mixer": T_MIXIN + T_MIXOUT, "cross": T_XKV + T_XQO, "pool": T_POOL,
         "nsa": T_NSAIN + T_NSAOUT, "blocknorm": 0, "finalnorm": 0}

COLS = {}


def _cols():
    at = 0
    for name, n in (("ones", 8), ("ffn0", 8), ("mix0", 8), ("crossn0", 8), ("memn0", 8), ("ffn1", 8),
                    ("ffn2", 8), ("mix1", 8), ("crossn1", 8), ("memn1", 8), ("ffn3", 8),
                    ("ffn4", 8), ("mix2", 8), ("crossn2", 8), ("memn2", 8), ("ffn5", 8),
                    ("ssd_norm", 8), ("subln", 1), ("conv_w", 64), ("conv_b", 16),
                    ("cmp_pos", 32)):
        COLS[name] = (at, n)
        at += n
    return at


NCOLS = _cols()
K_IDENT, K_TRIU, K_SEGMASK, K_CAUSAL, K_CMPMASK, K_ANYVIS, K_ONES, K_FLIP, NCONST = 0, 128, 256, 384, 640, 672, 674, 802, 930
R_DTB, R_ALOG, R_DSKIP, R_LAM, NROWS = 0, 16, 32, 48, 48 + 256

A_XN = 0
A_Z, A_XS, A_BT, A_CT, A_BTOK, A_XP, A_CV, A_XST, A_XDT = 2048, 4096, 6144, 7168, 8192, 8704, 9740, 10764, 11788
A_Q, A_K, A_V, A_BIAS, A_S, A_WT, A_MEM = 2048, 4096, 6144, 8192, 10240, 11264, 11776
A_YTMP = A_BTOK
A_SEG, A_XDTE, A_PREV = A_XST, A_XP, A_CV
A_TAB = 13000
A_BAND, A_ROWS = 8192, 4608
A_KC2, A_VC2, A_KS, A_KW, A_VS, A_VW = 4096, 5120, 6144, 7168, 8192, 8704
A_BLK, A_S3, A_WT3 = 9216, 9216, 10752
A_KCMP, A_VCMP, A_HIDC, A_W2, A_GATES = 12032, 12096, 12352, 12592, 13104
A_GATE, A_HID, A_DTW = 2048, 3072, 4096
ARENA = 13840


class Position:

    def __init__(self):
        self.tile = 0
        self.ffn = 0
        self.x = 0
        self.rstd = 0
        self.sum = 0
        self.turn = 0
        self.src = 0
        self.proj = 0
        self.layer = {"ffn": 0, "cross": 0}
        self.rows = 0
        self.unit = 0


def program(nc, weights, cols, consts, rows, rowsD, dtw, w2c, relb, onehot, band, x_in, mems, out, toep):
    total = sum(TILES[s] for s in STAGES)
    nt = weights.shape[0]
    ctx = ExitStack()
    with ctx:
        def sb(name, shape, dt=F32):
            return ctx.enter_context(nc.sbuf_tensor(name, shape, dt))

        def sem(name):
            return ctx.enter_context(nc.semaphore(name))

        raw = sb("raw", [P, RAW, 2048])
        w_hi = sb("w_hi", [P, SPL, 2048], F32R)
        w_lo = sb("w_lo", [P, SPL, 2048], F32R)
        x = sb("x", [P, TT, D])
        xT_hi = sb("xT_hi", [P, KC, S], F32R)
        xT_lo = sb("xT_lo", [P, KC, S], F32R)
        mT_hi = sb("mT_hi", [P, KC, S], F32R)
        mT_lo = sb("mT_lo", [P, KC, S], F32R)
        h_hi = mT_hi[:, 0:4, :].rearrange("p (a b) s -> p a b s", a=2)
        h_lo = mT_lo[:, 0:4, :].rearrange("p (a b) s -> p a b s", a=2)
        col = sb("col", [P, NCOLS])
        con = sb("con", [P, NCONST])
        row = sb("row", [P, NROWS])
        zeros = sb("zeros", [P, 512], BF16)
        sums = sb("sums", [P, 80])
        minus_half = sb("minus_half", [P, 16])
        small = sb("small", [P, 512])
        dtw_hi = sb("dtw_hi", [P, KC, 64], F32R)
        dtw_lo = sb("dtw_lo", [P, KC, 64], F32R)
        arena = sb("arena", [P, ARENA])
        PS = ctx.enter_context(nc.psum_tensor("PS", [P, 8, 512], F32))

        def area(at, *shape):
            n = int(np.prod(shape))
            v = arena[:, at:at + n]
            if len(shape) == 2:
                return v.rearrange("p (a b) -> p a b", a=shape[0])
            if len(shape) == 4:
                return v.rearrange("p (a b c d) -> p a b c d", a=shape[0], b=shape[1], c=shape[2])
            if len(shape) == 3:
                return v.rearrange("p (a b c) -> p a b c", a=shape[0], b=shape[1])
            return v

        xn = area(A_XN, TT, D)
        memx = area(A_MEM, TT, D)
        gate = area(A_GATE, 2, 2, S)
        hid = area(A_HID, 2, 2, S)
        dtw_raw = area(A_DTW, KC, 64)
        ident = con[:, K_IDENT:K_IDENT + P]

        nmax = small[:, 0:8].rearrange("p (a b) -> p a b", a=2)
        esum = small[:, 8:16].rearrange("p (a b) -> p a b", a=2)
        rsum = small[:, 16:24].rearrange("p (a b) -> p a b", a=2)

        neg_lam, subln2 = small[:, 28:29], small[:, 29:30]
        lam_e, lam_s, lam_p = small[:, 26:28], small[:, 24:26], small[:, 64:192]
        dt_x, dt_n, dt_e, dt_u, dt_r, dt_v, la, lc = (small[:, i:i + 32] for i in range(192, 448, 32))
        y_tmp = area(A_YTMP, 2, 256)
        to_end, from_start, a_exp = small[:, 448:464], small[:, 464:480], small[:, 480:496]

        def heads(v, n, w):
            return v.unsqueeze(2).broadcast_to([P, n, w])

        def blk_parts(i):
            return [m[:, 4 * i:4 * i + 4, :].rearrange("p a b -> p (a b)")[:, 0:960] for m in (mT_hi, mT_lo)]

        def column(name, c=0, n=1):
            at = COLS[name][0] + c
            return col[:, at:at + n]

        setup = sem("setup")
        setup_small = sem("setup_small")
        dtw_hi_ready = sem("dtw_hi_ready")
        dtw_ready = sem("dtw_ready")
        landed = [sem(f"landed{i}") for i in range(RAW)]
        hi_ready = sem("hi_ready")
        lo_ready = sem("lo_ready")
        tile_used = sem("tile_used")
        prep = sem("prep")
        silu_done = sem("silu_done")
        hidden = sem("hidden")
        hhi_ready = sem("hhi_ready")
        hlo_ready = sem("hlo_ready")
        first_sums = sem("first_sums")
        x_ready = sem("x_ready")
        sq_done = sem("sq_done")
        eps_added = sem("eps_added")
        rstd_ready = sem("rstd_ready")
        dve_step = sem("dve_step")
        act_step = sem("act_step")
        src_ready = sem("src_ready")
        turned = sem("turned")
        thi_ready = sem("thi_ready")
        tlo_ready = sem("tlo_ready")
        evac_done = sem("evac_done")
        side = sem("side")
        w2_landed = sem("w2_landed")
        cmp_ready = sem("cmp_ready")
        blk_full = sem("blk_full")
        blk_hi = sem("blk_hi")
        blk_ready = sem("blk_ready")
        cmp_done = sem("cmp_done")
        gates_done = sem("gates_done")
        gates_ready = sem("gates_ready")
        tab_landed = sem("tab_landed")
        tab_done = sem("tab_done")
        tab_ready = sem("tab_ready")
        tab_stored = sem("tab_stored")
        bias_landed = sem("bias_landed")
        bias_flipped = sem("bias_flipped")
        bias_ready = sem("bias_ready")
        lam_ready = sem("lam_ready")
        dt_done = sem("dt_done")
        dt_step = sem("dt_step")
        dt_act = sem("dt_act")
        la_ready = sem("la_ready")
        lc_done = sem("lc_done")
        lc_ready = sem("lc_ready")
        decay_ready = sem("decay_ready")
        conv_done = sem("conv_done")
        xbc_ready = sem("xbc_ready")
        xs_turned = sem("xs_turned")
        xs_ready = sem("xs_ready")
        xdt_ready = sem("xdt_ready")
        prev_done = sem("prev_done")
        prev_ready = sem("prev_ready")
        cb_done = sem("cb_done")
        seg_ready = sem("seg_ready")
        e_ready = sem("e_ready")
        m_ready = sem("m_ready")
        y_done = sem("y_done")
        yadd_done = sem("yadd_done")
        gated = sem("gated")
        mem_landed = sem("mem_landed")
        rows_landed = sem("rows_landed")
        logits_done = sem("logits_done")
        max_ready = sem("max_ready")
        exp_done = sem("exp_done")
        prob_ready = sem("prob_ready")
        prob_turned = sem("prob_turned")
        probT_ready = sem("probT_ready")
        pv_done = sem("pv_done")
        o_ready = sem("o_ready")
        stored = sem("stored")

        block = ctx.enter_context(nc.Block())

        @block.sync
        def _(sp):
            for m in range(TT):
                sp.dma_start(x[:, m, :], x_in[m]).then_inc(setup, 16)
            sp.dma_start(con[:], consts).then_inc(setup, 16)
            sp.dma_start(col[:], cols).then_inc(setup, 16)
            for n in range(RAW):
                sp.dma_start(raw[:, n, :], weights[n]).then_inc(landed[n], 16)
                if n == 1:
                    sp.dma_start(dtw_raw, dtw).then_inc(setup_small, 16)
            rounds = nt // RAW
            with sp.Fori(1, rounds) as r:
                for s in range(RAW):
                    sp.wait_ge(lo_ready, (r - 1) * RAW + s + 1)
                    sp.dma_start(raw[:, s, :], weights[bass.ds(r * RAW + s, 1)].rearrange("a p n -> (a p) n")
                                 ).then_inc(landed[s], 16)
            for n in range(rounds * RAW, nt):
                sp.wait_ge(lo_ready, n - RAW + 1)
                sp.dma_start(raw[:, n % RAW, :], weights[n]).then_inc(landed[n % RAW], 16)
            sp.wait_ge(x_ready, TT * len(STAGES))
            for m in range(TT):
                sp.dma_start(out[m], x[:, m, :]).then_inc(stored, 16)
            sp.wait_ge(stored, 16 * TT)

        @block.gpsimd
        def _(pool):
            pool.dma_start(row[:], rows.partition_broadcast(P)).then_inc(side, 16)
            pool.memset(minus_half[:], -0.5).then_inc(prep, 1)
            tab = area(A_TAB, 2, 384)
            pool.dma_start(tab[0:BUCKETS + 1, 0, :], onehot).then_inc(tab_landed, 16)
            pool.dma_start(arena[0:BUCKETS + 1, A_TAB + 768:A_TAB + 776], relb).then_inc(tab_landed, 16)
            pool.wait_ge(side, 16)
            pool.wait_ge(prep, 2)
            at = Position()

            def reciprocal_roots(n):
                v = sums[:, at.sum:at.sum + n]
                pool.wait_ge(sq_done, at.rstd + 1)
                pool.tensor_scalar(v, v, EPS, None, ALU.add).then_inc(eps_added, 1)
                pool.wait_ge(eps_added, at.rstd + 1)
                pool.tensor_tensor(v, v, minus_half[:, 0:n], ALU.pow).then_inc(rstd_ready, 1)
                at.rstd += 1
                at.sum += n

            def load_mem():
                src = mems[0 if at.layer["cross"] == 0 else 1]
                pool.dma_start(memx[:], src.rearrange("t p d -> p t d")).then_inc(mem_landed, 16)

            def load_rows(first, n):
                for i in range(n):
                    pool.dma_start(area(A_ROWS + i * D, D), rowsD[first + i].partition_broadcast(P)
                                   ).then_inc(rows_landed, 16)

            for i, stage in enumerate(STAGES):
                after = STAGES[i + 1] if i + 1 < len(STAGES) else None
                if stage == "ffn":
                    if after == "pool":
                        if at.x:
                            pool.wait_ge(x_ready, at.x)
                        pool.dma_start(area(A_BAND, TT * 4 * S), band).then_inc(rows_landed, 16)
                    if after in ("blocknorm", "finalnorm", "pool"):
                        if at.x:
                            pool.wait_ge(x_ready, at.x)
                        load_rows({"blocknorm": 0, "pool": 1, "finalnorm": 3}[after], 2 if after == "pool" else 1)
                    for m in range(TT):
                        reciprocal_roots(1)
                elif stage == "mixer":
                    for m in range(TT):
                        reciprocal_roots(1)
                    pool.wait_ge(tab_ready, 1)
                    pool.dma_start(toep, tab[0:DA_HEADS, 1, :]).then_inc(tab_stored, 16)
                    pool.wait_ge(tab_stored, 16)
                    pool.wait_ge(gated, 1)
                    pool.dma_start(area(A_BIAS, DA_HEADS, S),
                                   bass.AP(tensor=toep.tensor, offset=0, ap=[[1, P], [384, DA_HEADS], [1, S]])
                                   ).then_inc(bias_landed, 16)
                    reciprocal_roots(8)
                    if after == "cross":
                        load_mem()
                    reciprocal_roots(16)
                elif stage == "cross":
                    if STAGES[i - 1] != "mixer":
                        if at.x:
                            pool.wait_ge(x_ready, at.x)
                        load_mem()
                    at.layer["cross"] += 1
                    for m in range(2 * TT):
                        reciprocal_roots(1)
                elif stage in ("blocknorm", "finalnorm", "pool", "nsa"):
                    if stage == "nsa":
                        for half in range(2):
                            pool.dma_start(area(A_W2, 4, P)[:, :, half * 64:(half + 1) * 64],
                                           w2c.rearrange("p a c d -> p (a c) d")).then_inc(w2_landed, 16)
                    for m in range(TT):
                        reciprocal_roots(1)
                at.x += TT

        @block.tensor
        def _(pe):
            at = Position()

            def mm3(out, lh, ll, rh, rl, start, stop):
                pe.matmul(out, lh, rh, start=start, stop=False, skip_group_check=True)
                pe.matmul(out, lh, rl, start=False, stop=False, skip_group_check=True)
                return pe.matmul(out, ll, rh, start=False, stop=stop, skip_group_check=True)

            def next_proj(src, rows_out, fresh=None):
                if at.proj >= 4:
                    pe.wait_ge(evac_done, at.proj - 3)
                proj(at.tile, at.tile % SPL, 4 + at.proj % 4, src, rows_out, fresh)
                at.tile += 1
                at.proj += 1

            def next_accumulate(hi, lo, k0, start, stop):
                accumulate(at.tile, at.tile % SPL, hi, lo, k0, start, stop)
                at.tile += 1

            def proj(n, slot, bank, src, rows_out, fresh=None):
                hi, lo = (xT_hi, xT_lo) if src == "x" else (mT_hi, mT_lo)
                pe.wait_ge(lo_ready, n + 1)
                for part in range(2):
                    for k in range(KC):
                        if fresh is not None and part == 0:
                            pe.wait_ge(tlo_ready, fresh * KC + k + 1)
                        o = PS[:, bank, part * 256:(part + 1) * 256]
                        if rows_out:
                            a, b = hi[:, k, part * P:(part + 1) * P], lo[:, k, part * P:(part + 1) * P]
                            c = w_hi[:, slot, k * 256:(k + 1) * 256]
                            d = w_lo[:, slot, k * 256:(k + 1) * 256]
                        else:
                            w = k * 256 + part * P
                            a, b = w_hi[:, slot, w:w + P], w_lo[:, slot, w:w + P]
                            c, d = hi[:, k, :], lo[:, k, :]
                        last = mm3(o, a, b, c, d, k == 0, k == KC - 1)
                last.then_inc(tile_used, 1)

            def accumulate(n, slot, hi, lo, k0, start, stop):
                pe.wait_ge(lo_ready, n + 1)
                for m in range(TT):
                    for k in range(2):
                        for half in range(2):
                            w = k * D + half * 512
                            last = mm3(PS[:, 2 * m + half, :],
                                       hi[:, k0 + k, m * P:(m + 1) * P], lo[:, k0 + k, m * P:(m + 1) * P],
                                       w_hi[:, slot, w:w + 512], w_lo[:, slot, w:w + 512],
                                       start and k == 0, stop and k == 1)
                    if stop and m == 0:
                        last.then_inc(first_sums, 1)
                last.then_inc(tile_used, 1)

            def turn(src, ready=None):
                if ready:
                    pe.wait_ge(*ready)
                if at.turn:
                    pe.wait_ge(tlo_ready, KC * at.turn)
                for m in range(TT):
                    if not ready:
                        pe.wait_ge(src_ready, at.src + 1)
                        at.src += 1
                    for c in range(KC):
                        o = PS[:, c // 2, (c % 2) * 256 + m * P:(c % 2) * 256 + (m + 1) * P]
                        t = pe.transpose(o, src[:, m, c * P:(c + 1) * P], ident)
                        if m == TT - 1 and c % 2:
                            t.then_inc(turned, 1)
                at.turn += 1

            def ffn():
                n0, f0 = at.tile, at.ffn

                def gate_up(n, slot, p, fresh=None):
                    proj(n, slot, 4 + 2 * p, "x", False, fresh)
                    proj(n + 1, (slot + 1) % SPL, 5 + 2 * p, "x", False)

                def down(n, slot, p, i, stop):
                    pe.wait_ge(hlo_ready, f0 + i + 1)
                    accumulate(n, slot, h_hi[:, p], h_lo[:, p], 0, False, stop)

                gate_up(n0, n0 % SPL, 0, fresh=at.turn - 1)
                for b in range(4):
                    pe.matmul(PS[:, b, :], zeros[:, 0:P], zeros[:, :], start=True, stop=False,
                              skip_group_check=True)
                with pe.Fori(0, (FI - 1) // 2) as it:
                    for s in range(2):
                        n = it * 6 + (n0 + 2 + 3 * s)
                        gate_up(n, (n0 + 2) % SPL, (1 + s) % 2)
                        down(n + 2, (n0 + 4) % SPL, s, it * 2 + s, False)
                down(n0 + T_FFN - 1, (n0 + T_FFN - 1) % SPL, 0, FI - 1, True)
                at.tile += T_FFN
                at.ffn += FI

            def cross():
                turn(xn)
                for j in range(2):
                    next_proj("m", False, at.turn - 1 if j == 0 else None)
                turn(xn)
                for j in range(2):
                    next_proj("m", False)
                for j in range(4):
                    next_proj("m", True)
                for j in range(4):
                    next_proj("x", False)
                q, k, v = area(A_Q, KC, S), area(A_K, KC, S), area(A_V, TT, D)
                s, wT = area(A_S, 2, S), area(A_WT, 2, TT, P)
                units = [(h, t) for h in range(X_HEADS) for t in range(TT)]
                u0 = at.unit
                pe.wait_ge(evac_done, at.proj)
                def logits(i):
                    h, t = units[i]
                    if i >= 2:
                        pe.wait_ge(exp_done, u0 + i - 1)
                    for c in range(2):
                        last = pe.matmul(PS[:, i % 2, 0:S], q[:, 2 * h + c, t * P:(t + 1) * P],
                                         k[:, 2 * h + c, :], start=c == 0, stop=c == 1)
                    last.then_inc(logits_done, 1)

                logits(0)
                for i in range(len(units) + 2):
                    if i + 1 < len(units):
                        logits(i + 1)
                    if 1 <= i <= len(units):
                        j = i - 1
                        pe.wait_ge(prob_ready, u0 + j + 1)
                        if j >= 2:
                            pe.wait_ge(probT_ready, u0 + j - 1)
                        for b in range(TT):
                            last = pe.transpose(PS[:, 2 + j % 2, b * P:(b + 1) * P],
                                                s[:, j % 2, b * P:(b + 1) * P], ident)
                        last.then_inc(prob_turned, 1)
                    if i >= 2:
                        j = i - 2
                        h, t = units[j]
                        pe.wait_ge(probT_ready, u0 + j + 1)
                        if j >= 2:
                            pe.wait_ge(o_ready, u0 + j - 1)
                        for b in range(TT):
                            last = pe.matmul(PS[:, 4 + j % 2, 0:X_DIM], wT[:, j % 2, b, :],
                                             v[:, b, h * X_DIM:(h + 1) * X_DIM], start=b == 0, stop=b == TT - 1)
                        last.then_inc(pv_done, 1)
                at.unit += len(units)
                turn(xn, (o_ready, at.unit))
                pe.wait_ge(tlo_ready, KC * at.turn)
                for j in range(4):
                    next_accumulate(mT_hi, mT_lo, 2 * j, j == 0, j == 3)

            def pool_stage():
                bandv = area(A_BAND, TT, 4, S)
                pe.wait_ge(rows_landed, 16 * (at.rows + 3))
                at.rows += 3
                pe.wait_ge(tlo_ready, KC * at.turn)
                pe.wait_ge(src_ready, at.src + 2)
                at.src += 2
                for c in range(KC):
                    for m in range(TT):
                        t = pe.matmul(PS[:, c // 2, (c % 2) * 256:(c % 2 + 1) * 256], xn[:, m, c * P:(c + 1) * P],
                                      bandv[:, m, c // 2, :], start=m == 0, stop=m == TT - 1,
                                      skip_group_check=True)
                    if c % 2:
                        t.then_inc(turned, 1)
                at.turn += 1
                pe.wait_ge(tlo_ready, KC * at.turn)
                n, slot = at.tile, at.tile % SPL
                pe.wait_ge(lo_ready, n + 1)
                for m in range(TT):
                    for g in range(4):
                        for c in range(2):
                            k = 2 * g + c
                            last = mm3(PS[:, 2 * m + g // 2, (g % 2) * 256:(g % 2 + 1) * 256],
                                       xT_hi[:, k, m * P:(m + 1) * P], xT_lo[:, k, m * P:(m + 1) * P],
                                       w_hi[:, slot, k * 256:(k + 1) * 256], w_lo[:, slot, k * 256:(k + 1) * 256],
                                       c == 0, c == 1)
                last.then_inc(tile_used, 1)
                at.tile += 1

            def small_proj(out, col0, n):
                pe.wait_ge(dtw_ready, 1)
                for m in range(TT):
                    for k in range(KC):
                        last = mm3(out(m), xT_hi[:, k, m * P:(m + 1) * P], xT_lo[:, k, m * P:(m + 1) * P],
                                   dtw_hi[:, k, col0:col0 + n], dtw_lo[:, k, col0:col0 + n], k == 0, k == KC - 1)
                return last

            def mixer():
                turn(xn)
                for j in range(4):
                    next_proj("x", True, at.turn - 1 if j == 0 else None)
                small_proj(lambda m: PS[:, 3, m * 16:m * 16 + 16], 0, 16).then_inc(dt_done, 1)
                pe.wait_ge(tab_landed, 32)
                tab = area(A_TAB, 2, 384)
                pe.matmul(PS[0:DA_HEADS, 2, 0:384], arena[0:BUCKETS + 1, A_TAB + 768:A_TAB + 776],
                          tab[0:BUCKETS + 1, 0, :], start=True, stop=True).then_inc(tab_done, 1)
                xsT, btok = area(A_XST, 2, 2, S), area(A_BTOK, 4, P)
                bT, cT, prevT = area(A_BT, 4, S), area(A_CT, 4, S), area(A_PREV, 4, 256)
                xdt, xdte = area(A_XDT, TT, D), area(A_XDTE, 4, 256)
                triu, ones = con[:, K_TRIU:K_TRIU + P], con[:, K_ONES:K_ONES + P]
                for j in range(8):
                    next_proj("x", False)
                    if j == 0:
                        pe.wait_ge(la_ready, 1)
                        pe.matmul(PS[:, 3, 32:64], triu, la, start=True, stop=True, skip_group_check=True)
                        pe.matmul(PS[:, 3, 64:80], ones, la[:, 0:16], start=True, stop=True,
                                  skip_group_check=True).then_inc(lc_done, 1)
                    if 2 <= j < 6:
                        i = j - 2
                        pe.wait_ge(xbc_ready, i + 1)
                        if i >= 2:
                            pe.wait_ge(xs_ready, i - 1)
                        for m in range(TT):
                            for c in range(2):
                                last = pe.transpose(PS[:, i % 2, m * 256 + c * P:m * 256 + (c + 1) * P],
                                                    xsT[:, i % 2, c, m * P:(m + 1) * P], ident)
                        last.then_inc(xs_turned, 1)
                pe.wait_ge(xbc_ready, 6)
                pe.wait_ge(tab_ready, 1)
                for g in range(4):
                    last = pe.transpose(PS[:, 2, g * P:(g + 1) * P], bT[:, g, 0:P], ident)
                last.then_inc(xs_turned, 1)
                pe.wait_ge(xs_ready, 5)
                pe.wait_ge(xdt_ready, 1)
                for g in range(4):
                    last = pe.matmul(PS[:, 2 + g // 2, (g % 2) * 256:(g % 2 + 1) * 256], btok[:, g, :], xdte[:, g, :],
                                     start=True, stop=True, skip_group_check=True)
                last.then_inc(prev_done, 1)
                seg = area(A_SEG, 2, 4, P)
                pe.wait_ge(xbc_ready, 8)
                pe.wait_ge(evac_done, at.proj)
                for i in range(9):
                    if i < 8:
                        m, g = i // 4, i % 4
                        if i >= 2:
                            pe.wait_ge(m_ready, i - 1)
                        pe.matmul(PS[:, 4 + i % 2, 0:P], bT[:, g, m * P:(m + 1) * P], cT[:, g, m * P:(m + 1) * P],
                                  start=True, stop=True)
                        for r in range(4):
                            h = m * 16 + 4 * g + r
                            last = pe.matmul(PS[:, 6 + i % 2, r * P:(r + 1) * P], la[:, h:h + 1].broadcast_to([P, P]),
                                             triu, start=True, stop=True, skip_group_check=True)
                        last.then_inc(cb_done, 1)
                    if i >= 1:
                        j = i - 1
                        m, g = j // 4, j % 4
                        pe.wait_ge(m_ready, j + 1)
                        if j >= 2:
                            pe.wait_ge(yadd_done, j - 1)
                        for r in range(4):
                            h = 4 * g + r
                            last = pe.matmul(PS[:, j % 2, r * 64:(r + 1) * 64], seg[:, j % 2, r, :],
                                             xdt[:, m, h * 64:(h + 1) * 64], start=True, stop=True,
                                             skip_group_check=True)
                        if m == 1:
                            pe.wait_ge(prev_ready, 1)
                            last = pe.matmul(PS[:, 2 + j % 2, 0:256], cT[:, g, P:2 * P], prevT[:, g, :],
                                             start=True, stop=True)
                        last.then_inc(y_done, 1)
                for j in range(4):
                    next_proj("x", False)
                turn(xn)
                for j in range(4):
                    next_proj("x", False)
                for j in range(4):
                    next_proj("x", True)
                q, k, v = area(A_Q, KC, S), area(A_K, KC, S), area(A_V, TT, D)
                s, wT = area(A_S, 2, 2, S), area(A_WT, 2, 2, P)
                units = [(h, t) for h in range(DA_HEADS) for t in range(TT)]
                u0, n = at.unit, len(units)
                pe.wait_ge(evac_done, at.proj)
                pe.wait_ge(tlo_ready, KC * at.turn)
                pe.wait_ge(bias_landed, 16)
                for b in range(4):
                    last = pe.matmul(PS[:, b, :], con[:, K_FLIP:K_FLIP + P], area(A_BIAS, 4, 512)[:, b, :],
                                     start=True, stop=True)
                last.then_inc(bias_flipped, 1)
                pe.wait_ge(bias_ready, 1)

                def logits(i):
                    h, t = units[i]
                    if i >= 2:
                        pe.wait_ge(max_ready, u0 + i - 1)
                    for c in range(2):
                        last = pe.matmul(PS[:, 2 * (i % 2) + c, 0:(t + 1) * P],
                                         q[64 * c:64 * c + 64, h, t * P:(t + 1) * P],
                                         k[64 * c:64 * c + 64, h, 0:(t + 1) * P], start=True, stop=True)
                    last.then_inc(logits_done, 1)

                logits(0)
                for i in range(n + 2):
                    if i + 1 < n:
                        logits(i + 1)
                    if 1 <= i <= n:
                        j = i - 1
                        h, t = units[j]
                        pe.wait_ge(prob_ready, u0 + j + 1)
                        if j >= 2:
                            pe.wait_ge(probT_ready, u0 + j - 1)
                        for b in range(t + 1):
                            last = pe.transpose(PS[:, 4 + j % 2, b * P:(b + 1) * P], s[:, j % 2, 0, b * P:(b + 1) * P],
                                                ident)
                        last.then_inc(prob_turned, 1)
                    if i >= 2:
                        j = i - 2
                        h, t = units[j]
                        pe.wait_ge(probT_ready, u0 + j + 1)
                        if j >= 2:
                            pe.wait_ge(o_ready, u0 + j - 1)
                        for b in range(t + 1):
                            last = pe.matmul(PS[:, 6 + j % 2, 0:P], wT[:, j % 2, b, :], v[:, b, h * P:(h + 1) * P],
                                             start=b == 0, stop=b == t)
                        last.then_inc(pv_done, 1)
                at.unit += n
                turn(xn)
                pe.wait_ge(tlo_ready, KC * at.turn)
                for j in range(8):
                    hi, lo = (mT_hi, mT_lo) if j < 4 else (xT_hi, xT_lo)
                    next_accumulate(hi, lo, 2 * (j % 4), j == 0, j == 7)

            def nsa():
                turn(xn)
                for j in range(4):
                    next_proj("x", False, at.turn - 1 if j == 0 else None)
                small_proj(lambda m: PS[:, 0, m * 64:m * 64 + 48], 16, 48).then_inc(gates_done, 1)
                next_proj("x", False)
                next_proj("x", False)
                w2, hidc = area(A_W2, 2, 2, P), area(A_HIDC, 2, 2, 60)
                for i in range(2):
                    pe.wait_ge(blk_ready, i + 1)
                    bank = 3 - 3 * i
                    if i == 1:
                        pe.wait_ge(act_step, 1)
                    bh, bl = blk_parts(i)
                    for half in range(2):
                        slot = at.tile % SPL
                        pe.wait_ge(lo_ready, at.tile + 1)
                        for hc in range(2):
                            for t in range(8):
                                w, b = t * 256 + hc * P, (8 * half + t) * 60
                                last = mm3(PS[:, bank, hc * 64:hc * 64 + 60],
                                           w_hi[:, slot, w:w + P], w_lo[:, slot, w:w + P],
                                           bh[:, b:b + 60], bl[:, b:b + 60],
                                           half == 0 and hc == 0 and t == 0, half == 1 and t == 7)
                        last.then_inc(tile_used, 1)
                        at.tile += 1
                for j, rows_out in enumerate((False, True, False, True)):
                    next_proj("x", rows_out)
                    if j < 2:
                        pe.wait_ge(cmp_ready, j + 1)
                        pe.wait_ge(w2_landed, 32)
                        if j == 0:
                            for c in range(2):
                                last = pe.matmul(PS[:, 1, 0:60], w2[:, 0, c, :], hidc[:, 0, c, :], start=c == 0,
                                                 stop=c == 1)
                        else:
                            for g in range(NSA_KV):
                                for c in range(2):
                                    last = pe.matmul(PS[0:NCMP, 2, g * 64:(g + 1) * 64],
                                                     hidc[:, 1, c, g * NCMP:(g + 1) * NCMP], w2[:, 1, c, 0:64],
                                                     start=c == 0, stop=c == 1, skip_group_check=True)
                        last.then_inc(cmp_done, 1)
                q, ks, kw = area(A_Q, KC, S), area(A_KS, NSA_KV, S), area(A_KW, NSA_KV, S)
                vs, vw = area(A_VS, TT, 256), area(A_VW, TT, 256)
                kcmp, vcmp = area(A_KCMP, 64), area(A_VCMP, NSA_KV, 64)
                s, wT = area(A_S3, 2, 3, S), area(A_WT3, 2, 5, P)
                units = [(h, t) for h in range(NSA_HEADS) for t in range(TT)]
                u0, n = at.unit, len(units)
                pe.wait_ge(evac_done, at.proj)
                pe.wait_ge(cmp_ready, 4)
                pe.wait_ge(gates_ready, 1)

                def logits(i):
                    h, t = units[i]
                    g, a, nk = h // 4, 64 * (h % 2), (t + 1) * P
                    if i >= 2:
                        pe.wait_ge(max_ready, u0 + i - 1)
                    qh = q[a:a + 64, h // 2, t * P:(t + 1) * P]
                    pe.matmul(PS[:, i % 2, 0:nk], qh, ks[a:a + 64, g, 0:nk], start=True, stop=True,
                              skip_group_check=True)
                    pe.matmul(PS[:, i % 2, S:S + nk], qh, kw[a:a + 64, g, 0:nk], start=True, stop=True,
                              skip_group_check=True)
                    pe.matmul(PS[:, 2 + i % 2, 0:NCMP], qh, kcmp[a:a + 64, g * NCMP:(g + 1) * NCMP],
                              start=True, stop=True, skip_group_check=True).then_inc(logits_done, 1)

                logits(0)
                for i in range(n + 2):
                    if i + 1 < n:
                        logits(i + 1)
                    if 1 <= i <= n:
                        j = i - 1
                        h, t = units[j]
                        pe.wait_ge(prob_ready, u0 + j + 1)
                        if j >= 2:
                            pe.wait_ge(o_ready, u0 + j - 1)
                        for br in range(2):
                            for b in range(t + 1):
                                pe.transpose(PS[:, 4 + j % 2, (2 * br + b) * P:(2 * br + b + 1) * P],
                                             s[:, j % 2, 1 + br, b * P:(b + 1) * P], ident)
                        pe.transpose(PS[:, 6 + j % 2, 256:256 + P], s[:, j % 2, 0, 0:P], ident
                                     ).then_inc(prob_turned, 1)
                    if i >= 2:
                        j = i - 2
                        h, t = units[j]
                        g = h // 4
                        pe.wait_ge(probT_ready, u0 + j + 1)
                        o = PS[:, 6 + j % 2, 0:64]
                        for br, v in enumerate((vs, vw)):
                            for b in range(t + 1):
                                pe.matmul(o, wT[:, j % 2, 2 * br + b, :], v[:, b, g * 64:(g + 1) * 64],
                                          start=br == 0 and b == 0, stop=False, skip_group_check=True)
                        pe.matmul(o, wT[:, j % 2, 4, :], vcmp[:, g, :], start=False, stop=True,
                                  skip_group_check=True).then_inc(pv_done, 1)
                at.unit += n
                turn(xn, (o_ready, at.unit))
                pe.wait_ge(tlo_ready, KC * at.turn)
                for j in range(4):
                    next_accumulate(mT_hi, mT_lo, 2 * j, j == 0, j == 3)

            pe.wait_ge(setup, 64)
            pe.wait_ge(prep, 2)
            for stage in STAGES:
                if stage == "mixer":
                    mixer()
                if stage == "pool":
                    pool_stage()
                if stage == "nsa":
                    nsa()
                if stage in ("blocknorm", "finalnorm"):
                    at.rows += 1
                if stage == "ffn":
                    turn(xn)
                    ffn()
                elif stage == "cross":
                    cross()

        @block.scalar
        def _(act):
            at = Position()

            def split(n, slot, raw_slot, uses):
                act.wait_ge(landed[raw_slot], uses * 16)
                act.activation(w_hi[:, slot, :], raw[:, raw_slot, :], ACT.Copy).then_inc(hi_ready, 1)

            late, begun = [False], [False]

            def next_split():
                at.tile += 1
                split_behind()

            def split_behind():
                n = at.tile - 1 + SPL
                if n < total:
                    act.wait_ge(tile_used, n - SPL + 1)
                    split(n, n % SPL, n % RAW, n // RAW + 1)

            def late_split():
                if late[0]:
                    split_behind()
                elif at.tile == 0 and not begun[0]:
                    first_splits(1, SPL)
                    begun[0] = True
                late[0] = False

            def mean_square(src, wait):
                if at.turn:
                    act.wait_ge(turned, 4 * at.turn)
                for m in range(TT):
                    if wait:
                        act.wait_ge(x_ready, at.x - TT + m + 1)
                    act.activation(xn[:, m, :], src[:, m, :], ACT.Square, scale=1.0 / math.sqrt(D),
                                   accum_out=sums[:, at.sum:at.sum + 1]).then_inc(sq_done, 1)
                    at.sum += 1

            def turn(name, hi):
                if at.tile:
                    act.wait_ge(tile_used, at.tile)
                for c in range(KC):
                    act.wait_ge(turned, 4 * at.turn + c // 2 + 1)
                    w = column(name, c) if name != "subln2" else subln2
                    act.activation(hi[:, c, :], PS[:, c // 2, (c % 2) * 256:(c % 2 + 1) * 256], ACT.Copy,
                                   scale=w).then_inc(thi_ready, 1)
                at.turn += 1
                late_split()

            def ffn():
                n0, f0 = at.tile, at.ffn

                def silu(n, p):
                    act.wait_ge(tile_used, n + 1)
                    act.activation(gate[:, p].rearrange("p a b -> p (a b)"), PS[:, 4 + 2 * p, :],
                                   ACT.Silu).then_inc(silu_done, 1)

                def hidden_hi(p, i):
                    act.wait_ge(hidden, f0 + i + 1)
                    act.activation(h_hi[:, p], hid[:, p], ACT.Copy).then_inc(hhi_ready, 1)

                def loop_split(n, slot, raw_slot, uses, used):
                    act.wait_ge(tile_used, used)
                    split(n, slot, raw_slot, uses)

                silu(n0, 0)
                next_split()
                next_split()
                hidden_hi(0, 0)
                with act.Fori(0, (FI - 1) // 2) as it:
                    for s in range(2):
                        r = n0 + 2 + 3 * s

                        def ahead(j):
                            n = r + j + SPL
                            loop_split(None, n % SPL, n % RAW, it * (6 // RAW) + (n // RAW + 1), it * 6 + (r + j + 1))
                        silu(it * 6 + r, (1 + s) % 2)
                        ahead(0)
                        ahead(1)
                        hidden_hi((1 + s) % 2, it * 2 + (1 + s))
                        ahead(2)
                at.tile = n0 + T_FFN
                late[0] = True
                at.ffn += FI

            def evacuate(out, func=ACT.Copy, shape=None):
                act.wait_ge(tile_used, at.tile + 1)
                src = PS[:, 4 + at.proj % 4, :]
                if shape:
                    src = src.rearrange("p (a b) -> p a b", a=2)
                act.activation(out, src, func).then_inc(evac_done, 1)
                at.proj += 1
                next_split()

            def cross():
                act.wait_ge(mem_landed, 16 * (at.layer["cross"] + 1))
                q, k, v = area(A_Q, 4, 512), area(A_K, 4, 512), area(A_V, TT, D)
                s, wT = area(A_S, 2, S), area(A_WT, 2, S)
                mean_square(memx, False)
                turn(f"memn{at.layer['cross']}", mT_hi)
                mean_square(x, at.x > 0)
                for j in range(2):
                    evacuate(k[:, j, :])
                turn(f"crossn{at.layer['cross']}", xT_hi)
                for j in range(2, 4):
                    evacuate(k[:, j, :])
                for j in range(4):
                    evacuate(v[:, :, j * 256:(j + 1) * 256], shape=True)
                for j in range(4):
                    evacuate(q[:, j, :])
                u0, n = at.unit, X_HEADS * TT
                for i in range(n + 2):
                    if i < n:
                        if i >= 2:
                            act.wait_ge(prob_turned, u0 + i - 1)
                        act.wait_ge(max_ready, u0 + i + 1)
                        act.activation(s[:, i % 2, :], PS[:, i % 2, 0:S], ACT.Exp, bias=nmax[:, i % 2, 0:1],
                                       scale=X_DIM ** -0.5, accum_out=esum[:, i % 2, 0:1]).then_inc(exp_done, 1)
                    if 1 <= i <= n:
                        j = i - 1
                        act.wait_ge(prob_turned, u0 + j + 1)
                        if j >= 2:
                            act.wait_ge(pv_done, u0 + j - 1)
                        act.activation(wT[:, j % 2, :], PS[:, 2 + j % 2, 0:S], ACT.Copy).then_inc(probT_ready, 1)
                    if i >= 2:
                        j = i - 2
                        h, t = j // TT, j % TT
                        act.wait_ge(pv_done, u0 + j + 1)
                        act.activation(xn[:, t, h * X_DIM:(h + 1) * X_DIM], PS[:, 4 + j % 2, 0:X_DIM],
                                       ACT.Copy).then_inc(o_ready, 1)
                at.unit += n
                turn("ones", mT_hi)
                for j in range(3):
                    next_split()
                at.tile += 1
                late[0] = True
                at.layer["cross"] += 1
                at.x += TT

            def mixer():
                z, xp, cv = area(A_Z, TT, D), area(A_XP, 2, 2, S + 3), area(A_CV, 2, 2, S)
                xsT, xs, btok = area(A_XST, 2, 512), area(A_XS, TT, D), area(A_BTOK, 512)
                bT, cT, prevT = area(A_BT, 2, 512), area(A_CT, 2, 512), area(A_PREV, 2, 512)
                mean_square(x, at.x > 0)
                turn("mix0", xT_hi)
                for j in range(4):
                    evacuate(z[:, :, j * 256:(j + 1) * 256], ACT.Silu, shape=True)
                act.wait_ge(dt_step, 1)
                act.activation(lam_e, lam_s, ACT.Exp)
                act.activation(a_exp, row[:, R_ALOG:R_ALOG + 16], ACT.Exp)
                act.wait_ge(dt_step, 2)
                act.activation(dt_e, dt_n, ACT.Exp).then_inc(dt_act, 1)
                act.wait_ge(dt_step, 3)
                act.activation(dt_n, dt_u, ACT.Ln).then_inc(dt_act, 1)
                p0 = at.proj
                for j in range(9):
                    if j < 8:
                        if j >= 2:
                            act.wait_ge(conv_done, j - 1)
                        evacuate(xp[:, j % 2, :, 3:S + 3], shape=True)
                    if j >= 1:
                        i = j - 1
                        act.wait_ge(conv_done, i + 1)
                        if i < 4:
                            dst = xsT[:, i % 2, :]
                            if i >= 2:
                                act.wait_ge(xs_turned, i - 1)
                        else:
                            dst = (bT if i < 6 else cT)[:, i % 2, :]
                        act.activation(dst, cv[:, i % 2].rearrange("p a b -> p (a b)"),
                                       ACT.Silu).then_inc(xbc_ready, 1)
                    if 3 <= j < 7:
                        i = j - 3
                        act.wait_ge(xs_turned, i + 1)
                        act.activation(xs[:, :, i * 256:(i + 1) * 256],
                                       PS[:, i % 2, :].rearrange("p (a b) -> p a b", a=2), ACT.Copy
                                       ).then_inc(xs_ready, 1)
                act.wait_ge(xs_turned, 5)
                act.activation(btok, PS[:, 2, :], ACT.Copy).then_inc(xs_ready, 1)
                act.wait_ge(lc_ready, 1)
                act.activation(to_end, to_end, ACT.Exp)
                act.activation(from_start, lc[:, 16:32], ACT.Exp).then_inc(decay_ready, 1)
                act.wait_ge(prev_done, 1)
                act.activation(prevT, PS[:, 2:4, :], ACT.Copy).then_inc(prev_ready, 1)
                seg = area(A_SEG, 2, 512)
                for i in range(8):
                    act.wait_ge(seg_ready, i + 1)
                    act.activation(seg[:, i % 2, :], seg[:, i % 2, :], ACT.Exp).then_inc(e_ready, 1)
                act.wait_ge(gated, 1)
                for m in range(TT):
                    for g in range(4):
                        v = slice(g * 256, (g + 1) * 256)
                        last = act.activation(area(A_XDT, TT, D)[:, m, v], xn[:, m, v], ACT.Square, scale=1.0 / 16,
                                              accum_out=sums[:, at.sum:at.sum + 1])
                        at.sum += 1
                last.then_inc(sq_done, 1)
                q, k, v = area(A_Q, 4, 512), area(A_K, 4, 512), area(A_V, TT, D)
                for j in range(4):
                    evacuate(q[:, j, :])
                turn("ssd_norm", mT_hi)
                for j in range(4):
                    evacuate(k[:, j, :])
                for j in range(4):
                    evacuate(v[:, :, j * 256:(j + 1) * 256], shape=True)
                act.wait_ge(bias_flipped, 1)
                act.activation(area(A_BIAS, 4, 512), PS[:, 0:4, :], ACT.Copy).then_inc(bias_ready, 1)
                s, wT = area(A_S, 2, 2, S), area(A_WT, 2, 256)
                units = [(h, t) for h in range(DA_HEADS) for t in range(TT)]
                u0, n = at.unit, len(units)
                for i in range(n + 2):
                    if i < n:
                        h, t = units[i]
                        act.wait_ge(max_ready, u0 + i + 1)
                        for c in range(2):
                            v = s[:, i % 2, c, 0:(t + 1) * P]
                            last = act.activation(v, v, ACT.Exp, bias=nmax[:, i % 2, c:c + 1],
                                                  accum_out=esum[:, i % 2, c:c + 1])
                        last.then_inc(exp_done, 1)
                    if 1 <= i <= n:
                        j = i - 1
                        h, t = units[j]
                        act.wait_ge(prob_turned, u0 + j + 1)
                        if j >= 2:
                            act.wait_ge(pv_done, u0 + j - 1)
                        act.activation(wT[:, j % 2, 0:(t + 1) * P], PS[:, 4 + j % 2, 0:(t + 1) * P],
                                       ACT.Copy).then_inc(probT_ready, 1)
                    if i >= 2:
                        j = i - 2
                        h, t = units[j]
                        act.wait_ge(pv_done, u0 + j + 1)
                        act.activation(xn[:, t, h * P:(h + 1) * P], PS[:, 6 + j % 2, 0:P],
                                       ACT.Copy).then_inc(o_ready, 1)
                at.unit += n
                at.sum += 16
                turn("subln2", xT_hi)
                for j in range(7):
                    next_split()
                at.tile += 1
                late[0] = True
                at.x += TT

            def duplicate(dst, shift):
                act.wait_ge(tile_used, at.tile + 1)
                for half in range(2):
                    src = PS[64 * half:64 * half + 64, 4 + at.proj % 4, :].rearrange("p (a b) -> p a b", a=2)
                    d = dst.rearrange("p (a c) s -> p a c s", c=2)
                    act.activation(d[0:64, :, half, :], src, ACT.Copy)
                    last = act.activation(d[64:128, :, half, 0:S - shift], src[:, :, shift:S], ACT.Copy)
                last.then_inc(evac_done, 1)
                at.proj += 1
                next_split()

            def nsa():
                q, kc, vc = area(A_Q, 4, 512), area(A_KC2, NSA_KV, S), area(A_VC2, NSA_KV, S)
                ks, kw = area(A_KS, NSA_KV, S), area(A_KW, NSA_KV, S)
                vs, vw = area(A_VS, TT, 256), area(A_VW, TT, 256)
                mean_square(x, at.x > 0)
                turn("mix2", xT_hi)
                for j in range(4):
                    evacuate(q[:, j, :])
                act.wait_ge(gates_done, 1)
                act.activation(area(A_GATES, TT, 48), PS[:, 0, 0:128].rearrange("p (a b) -> p a b", a=2)[:, :, 0:48],
                               ACT.Sigmoid).then_inc(act_step, 1)
                duplicate(kc, 1)
                duplicate(vc, 1)
                blk = area(A_BLK, 2, 960)
                for i in range(2):
                    act.wait_ge(blk_full, i + 1)
                    act.activation(blk_parts(i)[0], blk[:, i, :], ACT.Copy).then_inc(blk_hi, 1)
                for i in range(2):
                    next_split()
                    act.wait_ge(tile_used, at.tile + 1)
                    act.activation(area(A_HIDC, 2, 2, 60)[:, i], PS[:, 3 - 3 * i, 0:128].rearrange("p (a b) -> p a b", a=2)[:, :, 0:60],
                                   ACT.Gelu_apprx_tanh).then_inc(cmp_ready, 1)
                    next_split()
                duplicate(ks, 0)
                act.wait_ge(cmp_done, 1)
                act.activation(area(A_KCMP, 64)[:, 0:60], PS[:, 1, 0:60], ACT.Copy).then_inc(cmp_ready, 1)
                evacuate(vs, shape=True)
                act.wait_ge(cmp_done, 2)
                act.activation(area(A_VCMP, NSA_KV, 64)[0:NCMP], PS[0:NCMP, 2, 0:256].rearrange("p (a b) -> p a b", a=4),
                               ACT.Copy).then_inc(cmp_ready, 1)
                duplicate(kw, 0)
                evacuate(vw, shape=True)
                s, wT = area(A_S3, 2, 3, S), area(A_WT3, 2, 5, P)
                units = [(h, t) for h in range(NSA_HEADS) for t in range(TT)]
                u0, n = at.unit, len(units)
                for i in range(n + 2):
                    if i < n:
                        h, t = units[i]
                        act.wait_ge(max_ready, u0 + i + 1)
                        for br, nk in enumerate((NCMP, (t + 1) * P, (t + 1) * P)):
                            v = s[:, i % 2, br, 0:nk]
                            last = act.activation(v, v, ACT.Exp, bias=nmax[:, i % 2, br:br + 1],
                                                  accum_out=esum[:, i % 2, br:br + 1])
                        last.then_inc(exp_done, 1)
                    if 1 <= i <= n:
                        j = i - 1
                        h, t = units[j]
                        act.wait_ge(prob_turned, u0 + j + 1)
                        if j >= 2:
                            act.wait_ge(pv_done, u0 + j - 1)
                        nb = t + 1
                        act.activation(wT[:, j % 2, 0:4, :].rearrange("p (a b) c -> p a b c", a=2)[:, :, 0:nb, :],
                                       PS[:, 4 + j % 2, :].rearrange("p (a b c) -> p a b c", a=2, b=2)[:, :, 0:nb, :],
                                       ACT.Copy)
                        act.activation(wT[:, j % 2, 4, :], PS[:, 6 + j % 2, 256:256 + P],
                                       ACT.Copy).then_inc(probT_ready, 1)
                    if i >= 2:
                        j = i - 2
                        h, t = units[j]
                        act.wait_ge(pv_done, u0 + j + 1)
                        act.activation(xn[:, t, h * 64:(h + 1) * 64], PS[:, 6 + j % 2, 0:64],
                                       ACT.Copy).then_inc(o_ready, 1)
                at.unit += n
                turn("ones", mT_hi)
                for j in range(3):
                    next_split()
                at.tile += 1
                late[0] = True
                at.x += TT

            act.wait_ge(setup, 64)

            def first_splits(a, b):
                for n in range(a, b):
                    split(n, n % SPL, n % RAW, 1)
                if a == 0:
                    return
                act.wait_ge(setup_small, 16)
                act.activation(dtw_hi[:], dtw_raw, ACT.Copy).then_inc(dtw_hi_ready, 1)
            for stage in STAGES:
                if stage == "mixer":
                    mixer()
                if stage == "cross":
                    cross()
                if stage == "nsa":
                    nsa()
                if stage == "pool":
                    mean_square(x, at.x > 0)
                    turn("mix1", xT_hi)
                    next_split()
                    at.x += TT
                if stage in ("blocknorm", "finalnorm"):
                    mean_square(x, at.x > 0)
                    at.x += TT
                if stage == "ffn":
                    mean_square(x, at.x > 0)
                    if at.tile == 0:
                        first_splits(0, 1)
                    turn(f"ffn{at.layer['ffn']}", xT_hi)
                    ffn()
                    at.layer["ffn"] += 1
                    at.x += TT

        @block.vector
        def _(dve):
            at = Position()
            steps = [0]

            def chain(instruction):
                steps[0] += 1
                instruction.then_inc(dve_step, 1)
                dve.wait_ge(dve_step, steps[0])

            def split(n, slot, raw_slot):
                dve.wait_ge(hi_ready, n + 1)
                dve.tensor_tensor(w_lo[:, slot, :], raw[:, raw_slot, :], w_hi[:, slot, :],
                                  ALU.subtract).then_inc(lo_ready, 1)

            late, begun = [False], [False]

            def next_split():
                at.tile += 1
                split_behind()

            def split_behind():
                n = at.tile - 1 + SPL
                if n < total:
                    split(n, n % SPL, n % RAW)

            def late_split():
                if late[0]:
                    split_behind()
                elif at.tile == 0 and not begun[0]:
                    first_splits(1, SPL)
                    begun[0] = True
                late[0] = False

            def normalize(src, dst):
                for m in range(TT):
                    dve.wait_ge(rstd_ready, at.rstd + 1)
                    dve.tensor_scalar(dst[:, m, :], src[:, m, :], sums[:, at.sum:at.sum + 1], None,
                                      ALU.mult).then_inc(src_ready, 1)
                    at.rstd += 1
                    at.sum += 1

            def turn(name, hi, lo):
                for c in range(KC):
                    dve.wait_ge(thi_ready, KC * at.turn + 2 * (c // 2 + 1))
                    w = column(name, c) if name != "subln2" else subln2
                    dve.scalar_tensor_tensor(lo[:, c, :], PS[:, c // 2, (c % 2) * 256:(c % 2 + 1) * 256], w,
                                             hi[:, c, :], ALU.mult, ALU.subtract).then_inc(tlo_ready, 1)
                at.turn += 1
                late_split()

            def residual(factor):
                at.layer["sums"] = at.layer.get("sums", 0) + 1
                for m in range(TT):
                    if m == 0:
                        dve.wait_ge(first_sums, at.layer["sums"])
                    else:
                        dve.wait_ge(tile_used, at.tile)
                    u = dve.scalar_tensor_tensor(x[:, m, :], PS[:, 2 * m:2 * m + 2, :].rearrange("p a b -> p (a b)"),
                                                 factor, x[:, m, :], ALU.mult, ALU.add)
                    u.then_inc(x_ready, 1)
                at.x += TT

            def ffn():
                n0, f0 = at.tile, at.ffn

                def product(n, p, i):
                    dve.wait_ge(tile_used, n + 2)
                    dve.wait_ge(silu_done, f0 + i + 1)
                    dve.tensor_tensor(hid[:, p].rearrange("p a b -> p (a b)"), PS[:, 5 + 2 * p, :],
                                      gate[:, p].rearrange("p a b -> p (a b)"),
                                      ALU.mult).then_inc(hidden, 1)

                def hidden_lo(p, i):
                    dve.wait_ge(hhi_ready, f0 + i + 1)
                    dve.tensor_tensor(h_lo[:, p], hid[:, p], h_hi[:, p], ALU.subtract).then_inc(hlo_ready, 1)

                next_split()
                product(n0, 0, 0)
                next_split()
                hidden_lo(0, 0)
                with dve.Fori(0, (FI - 1) // 2) as it:
                    for s in range(2):
                        r = n0 + 2 + 3 * s

                        def ahead(j):
                            n = r + j + SPL
                            split(it * 6 + n, n % SPL, n % RAW)
                        p = (1 + s) % 2
                        ahead(0)
                        product(it * 6 + r, p, it * 2 + (1 + s))
                        ahead(1)
                        hidden_lo(p, it * 2 + (1 + s))
                        ahead(2)
                at.tile = n0 + T_FFN
                late[0] = True
                at.ffn += FI
                residual(0.5)

            def mixer():
                xp, cv = area(A_XP, 2, 2, S + 3), area(A_CV, 2, 2, S)
                xs, xdt, z = area(A_XS, TT, D), area(A_XDT, TT, D), area(A_Z, TT, D)
                dve.wait_ge(side, 16)
                v = row[:, R_LAM:R_LAM + 256].rearrange("p (a b c) -> p a b c", a=2, b=2)
                lp = lam_p.rearrange("p (a b) -> p a b", a=2)
                chain(dve.tensor_tensor(lp, v[:, :, 0, :], v[:, :, 1, :], ALU.mult))
                dve.tensor_reduce(lam_s, lp, AX_X, ALU.add).then_inc(dt_step, 1)
                chain(dve.tensor_scalar(subln2, column("subln"), 1.0 - LAMBDA_INIT, None, ALU.mult))
                normalize(x, xn)
                turn("mix0", xT_hi, xT_lo)
                for c in range(2):
                    chain(dve.memset(xp[:, c, :, 0:3], 0.0))
                for j in range(4):
                    next_split()
                dve.wait_ge(dt_done, 1)
                chain(dve.tensor_tensor(dt_x.rearrange("p (a b) -> p a b", a=2),
                                        PS[:, 3, 0:32].rearrange("p (a b) -> p a b", a=2),
                                        row[:, R_DTB:R_DTB + 16].unsqueeze(1).broadcast_to([P, 2, 16]), ALU.add))
                chain(dve.tensor_scalar(dt_n, dt_x, -1.0, None, ALU.mult))
                dve.tensor_tensor(dt_n, dt_n, dt_x, ALU.min).then_inc(dt_step, 1)
                dve.wait_ge(dt_act, 1)
                chain(dve.tensor_scalar(dt_u, dt_e, 1.0, None, ALU.add))
                dve.tensor_scalar(dt_v, dt_u, 1.0, None, ALU.subtract).then_inc(dt_step, 1)
                dve.wait_ge(dt_step, 3)
                chain(dve.tensor_tensor(dt_v, dt_e, dt_v, ALU.subtract))
                chain(dve.reciprocal(dt_r, dt_u))
                chain(dve.tensor_tensor(dt_v, dt_v, dt_r, ALU.mult))
                chain(dve.scalar_tensor_tensor(dt_v, dt_x, 0.0, dt_v, ALU.max, ALU.add))
                dve.wait_ge(dt_act, 2)
                chain(dve.tensor_tensor(dt_v, dt_v, dt_n, ALU.add))
                dve.scalar_tensor_tensor(la.rearrange("p (a b) -> p a b", a=2), dt_v.rearrange("p (a b) -> p a b", a=2),
                                         -1.0, a_exp.unsqueeze(1).broadcast_to([P, 2, 16]),
                                         ALU.mult, ALU.mult).then_inc(la_ready, 1)
                chain(dve.tensor_tensor(neg_lam, lam_e[:, 1:2], lam_e[:, 0:1], ALU.subtract))
                chain(dve.tensor_scalar(neg_lam, neg_lam, -LAMBDA_INIT, None, ALU.add))
                dve.wait_ge(tab_done, 1)
                dve.tensor_copy(area(A_TAB, 2, 384)[0:DA_HEADS, 1, :], PS[0:DA_HEADS, 2, 0:384]).then_inc(tab_ready, 1)
                for j in range(8):
                    next_split()
                    dve.wait_ge(evac_done, at.proj + 4 + j + 1)
                    if j >= 2:
                        dve.wait_ge(xbc_ready, j - 1)
                    for tap in range(CONV_W):
                        for c in range(2):
                            w = column("conv_w", tap * 16 + 2 * j + c)
                            o, i = cv[:, j % 2, c, :], xp[:, j % 2, c, tap:tap + S]
                            if tap == 0:
                                last = dve.tensor_scalar(o, i, w, column("conv_b", 2 * j + c), ALU.mult, ALU.add)
                            else:
                                last = dve.scalar_tensor_tensor(o, i, w, o, ALU.mult, ALU.add)
                        if tap < CONV_W - 1:
                            chain(last)
                    last.then_inc(conv_done, 1)
                at.proj += 12
                dve.wait_ge(lc_done, 1)
                chain(dve.tensor_copy(lc, PS[:, 3, 32:64]))
                dve.tensor_tensor(to_end, PS[:, 3, 64:80], lc[:, 0:16], ALU.subtract).then_inc(lc_ready, 1)
                dve.wait_ge(xs_ready, 4)
                dve.wait_ge(tab_stored, 16)
                dve.wait_ge(decay_ready, 1)
                for m in range(TT):
                    xh = xs[:, m, :].rearrange("p (a b) -> p a b", a=16)
                    last = dve.tensor_tensor(xdt[:, m, :].rearrange("p (a b) -> p a b", a=16), xh,
                                             heads(dt_v[:, 16 * m:16 * m + 16], 16, 64), ALU.mult)
                    if m == 0:
                        chain(last)
                        dve.tensor_tensor(area(A_XDTE, 16, 64), xdt[:, 0, :].rearrange("p (a b) -> p a b", a=16),
                                          heads(to_end, 16, 64), ALU.mult).then_inc(xdt_ready, 1)
                    last = dve.tensor_tensor(xn[:, m, :].rearrange("p (a b) -> p a b", a=16), xh,
                                             heads(row[:, R_DSKIP:R_DSKIP + 16], 16, 64), ALU.mult)
                chain(last)
                seg = area(A_SEG, 2, 4, P)
                for i in range(10):
                    if i < 8:
                        m, g = i // 4, i % 4
                        dve.wait_ge(cb_done, i + 1)
                        if i >= 2:
                            dve.wait_ge(y_done, i - 1)
                        for r in range(4):
                            h = m * 16 + 4 * g + r
                            last = dve.scalar_tensor_tensor(seg[:, i % 2, r, :], PS[:, 6 + i % 2, r * P:(r + 1) * P],
                                                            lc[:, h:h + 1], con[:, K_SEGMASK:K_SEGMASK + P],
                                                            ALU.subtract, ALU.add)
                        last.then_inc(seg_ready, 1)
                    if 1 <= i <= 8:
                        j = i - 1
                        dve.wait_ge(e_ready, j + 1)
                        dve.tensor_tensor(seg[:, j % 2], seg[:, j % 2],
                                          PS[:, 4 + j % 2, 0:P].unsqueeze(1).broadcast_to([P, 4, P]),
                                          ALU.mult).then_inc(m_ready, 1)
                    if i >= 2:
                        j = i - 2
                        m, g = j // 4, j % 4
                        dve.wait_ge(y_done, j + 1)
                        v = xn[:, m, g * 256:(g + 1) * 256]
                        last = dve.tensor_tensor(v, v, PS[:, j % 2, 0:256], ALU.add)
                        if m == 1:
                            t = y_tmp[:, j % 2]
                            chain(dve.tensor_tensor(t.rearrange("p (a b) -> p a b", a=4),
                                                    PS[:, 2 + j % 2, 0:256].rearrange("p (a b) -> p a b", a=4),
                                                    heads(from_start[:, 4 * g:4 * g + 4], 4, 64), ALU.mult))
                            last = dve.tensor_tensor(v, v, t, ALU.add)
                        last.then_inc(yadd_done, 1)
                dve.wait_ge(yadd_done, 8)
                for m in range(TT):
                    last = dve.tensor_tensor(xn[:, m, :], xn[:, m, :], z[:, m, :], ALU.mult)
                last.then_inc(gated, 1)
                dve.wait_ge(gated, 1)
                dve.wait_ge(rstd_ready, at.rstd + 1)
                for m in range(TT):
                    v = xn[:, m, :].rearrange("p (a b) -> p a b", a=4)
                    dve.tensor_tensor(v, v, heads(sums[:, at.sum + 4 * m:at.sum + 4 * m + 4], 4, 256),
                                      ALU.mult).then_inc(src_ready, 1)
                at.rstd += 1
                at.sum += 8
                for j in range(4):
                    next_split()
                turn("ssd_norm", mT_hi, mT_lo)
                for j in range(8):
                    next_split()
                at.proj += 12
                s, bias = area(A_S, 2, 2, S), area(A_BIAS, DA_HEADS, S)
                units = [(h, t) for h in range(DA_HEADS) for t in range(TT)]
                u0, n = at.unit, len(units)
                dve.wait_ge(bias_ready, 1)
                for i in range(n + 1):
                    if i < n:
                        h, t = units[i]
                        nk, p = (t + 1) * P, i % 2
                        dve.wait_ge(logits_done, u0 + i + 1)
                        if i >= 2:
                            dve.wait_ge(prob_turned, u0 + i - 1)
                        b = bias[:, h, (1 - t) * P:(1 - t) * P + nk]
                        chain(dve.scalar_tensor_tensor(s[:, p, :, 0:nk], PS[:, 2 * p:2 * p + 2, 0:nk], DA_DIM ** -0.5,
                                                       b.unsqueeze(1).broadcast_to([P, 2, nk]), ALU.mult, ALU.add))
                        dve.tensor_reduce(nmax[:, p, 0:2], s[:, p, :, 0:nk], AX_X, ALU.max,
                                          negate=True).then_inc(max_ready, 1)
                    if i >= 1:
                        j = i - 1
                        h, t = units[j]
                        nk, p = (t + 1) * P, j % 2
                        dve.wait_ge(exp_done, u0 + j + 1)
                        chain(dve.reciprocal(rsum[:, p, 0:2], esum[:, p, 0:2]))
                        dve.tensor_scalar(s[:, p, 0, 0:nk], s[:, p, 0, 0:nk], rsum[:, p, 0:1], None, ALU.mult)
                        chain(dve.tensor_tensor(rsum[:, p, 2:3], rsum[:, p, 1:2], neg_lam, ALU.mult))
                        dve.scalar_tensor_tensor(s[:, p, 0, 0:nk], s[:, p, 1, 0:nk], rsum[:, p, 2:3],
                                                 s[:, p, 0, 0:nk], ALU.mult, ALU.add).then_inc(prob_ready, 1)
                at.unit += n
                dve.wait_ge(o_ready, at.unit)
                sq = area(A_K, TT, D)
                chain(dve.scalar_tensor_tensor(sq, xn, 1.0 / (2 * DA_DIM), xn, ALU.mult, ALU.mult))
                dve.tensor_reduce(sums[:, at.sum:at.sum + 16], sq.rearrange("p a (b c) -> p (a b) c", b=DA_HEADS),
                                  AX_X, ALU.add).then_inc(sq_done, 1)
                dve.wait_ge(rstd_ready, at.rstd + 1)
                for m in range(TT):
                    v = xn[:, m, :].rearrange("p (a b) -> p a b", a=DA_HEADS)
                    dve.tensor_tensor(v, v, heads(sums[:, at.sum + 8 * m:at.sum + 8 * m + 8], 8, 2 * DA_DIM),
                                      ALU.mult).then_inc(src_ready, 1)
                at.rstd += 1
                at.sum += 16
                turn("subln2", xT_hi, xT_lo)
                for j in range(7):
                    next_split()
                at.tile += 1
                late[0] = True
                residual(1.0)

            def pool_stage():
                bias, scale = area(A_ROWS, D), area(A_ROWS + D, D)
                normalize(x, xn)
                turn("mix1", xT_hi, xT_lo)
                next_split()
                at.rows += 3
                dve.wait_ge(rows_landed, 16 * at.rows)
                dve.wait_ge(tile_used, at.tile)
                for m in range(TT):
                    y = PS[:, 2 * m:2 * m + 2, :].rearrange("p a b -> p (a b)")
                    chain(dve.tensor_tensor(xn[:, m, :], y, bias, ALU.add))
                    chain(dve.tensor_tensor(xn[:, m, :], xn[:, m, :], scale, ALU.mult))
                    dve.tensor_tensor(x[:, m, :], x[:, m, :], xn[:, m, :], ALU.add).then_inc(x_ready, 1)
                at.x += TT

            def nsa():
                chain(dve.memset(area(A_VCMP, 256), 0.0))
                normalize(x, xn)
                turn("mix2", xT_hi, xT_lo)
                for j in range(6):
                    next_split()
                blk = area(A_BLK, 2, 16, 4, NCMP)
                for i, c2 in enumerate((A_KC2, A_VC2)):
                    dve.wait_ge(evac_done, at.proj + 5 + i)
                    src = area(c2, NSA_KV, S)
                    pos = column("cmp_pos", 16 * i, 16)
                    for t in range(16):
                        last = dve.tensor_scalar(blk[:, i, t], src[:, :, 2 * t:2 * t + 16 * (NCMP - 1) + 1:16],
                                                 pos[:, t:t + 1], None, ALU.add)
                    last.then_inc(blk_full, 1)
                full = area(A_BLK, 2, 960)
                for i in range(2):
                    hi, lo = blk_parts(i)
                    dve.wait_ge(blk_hi, i + 1)
                    dve.tensor_tensor(lo, full[:, i, :], hi, ALU.subtract).then_inc(blk_ready, 1)
                dve.wait_ge(act_step, 1)
                gt = area(A_GATES, TT, 48)
                for m in range(TT):
                    v = gt[:, m, 0:48:3]
                    last = dve.tensor_scalar(v, v, con[:, K_ANYVIS + m:K_ANYVIS + m + 1], None, ALU.mult)
                last.then_inc(gates_ready, 1)
                dve.wait_ge(gates_ready, 1)
                for j in range(8):
                    next_split()
                at.proj += 10
                s = area(A_S3, 2, 3, S)
                dve.wait_ge(blk_ready, 2)
                for p in range(2):
                    chain(dve.memset(s[:, p, 0, 0:P], 0.0))
                units = [(h, t) for h in range(NSA_HEADS) for t in range(TT)]
                u0, n = at.unit, len(units)
                for i in range(n + 1):
                    if i < n:
                        h, t = units[i]
                        nk, p = (t + 1) * P, i % 2
                        dve.wait_ge(logits_done, u0 + i + 1)
                        if i >= 2:
                            dve.wait_ge(prob_turned, u0 + i - 1)
                        mask = con[:, K_CAUSAL + (2 - t - 1) * P:K_CAUSAL + 2 * P]
                        dve.scalar_tensor_tensor(s[:, p, 1:3, 0:nk], PS[:, p, :].rearrange("p (a b) -> p a b", a=2)[:, :, 0:nk],
                                                 NSA_DIM ** -0.5, mask.unsqueeze(1).broadcast_to([P, 2, nk]),
                                                 ALU.mult, ALU.add)
                        chain(dve.scalar_tensor_tensor(s[:, p, 0, 0:NCMP], PS[:, 2 + p, 0:NCMP], NSA_DIM ** -0.5,
                                                       con[:, K_CMPMASK + 16 * t:K_CMPMASK + 16 * t + NCMP],
                                                       ALU.mult, ALU.add))
                        dve.tensor_reduce(nmax[:, p, 1:3], s[:, p, 1:3, 0:nk], AX_X, ALU.max, negate=True)
                        dve.tensor_reduce(nmax[:, p, 0:1], s[:, p, 0, 0:NCMP], AX_X, ALU.max,
                                          negate=True).then_inc(max_ready, 1)
                    if i >= 1:
                        j = i - 1
                        h, t = units[j]
                        p, nk = j % 2, (t + 1) * P
                        dve.wait_ge(exp_done, u0 + j + 1)
                        chain(dve.reciprocal(rsum[:, p, 0:3], esum[:, p, 0:3]))
                        chain(dve.tensor_tensor(rsum[:, p, 0:3], rsum[:, p, 0:3], gt[:, t, 3 * h:3 * h + 3], ALU.mult))
                        for br, m in enumerate((NCMP, nk, nk)):
                            v = s[:, p, br, 0:m]
                            last = dve.tensor_scalar(v, v, rsum[:, p, br:br + 1], None, ALU.mult)
                        last.then_inc(prob_ready, 1)
                at.unit += n
                turn("ones", mT_hi, mT_lo)
                for j in range(3):
                    next_split()
                at.tile += 1
                late[0] = True
                residual(1.0)

            def row_norm():
                at.rows += 1
                dve.wait_ge(rows_landed, 16 * at.rows)
                for m in range(TT):
                    dve.wait_ge(rstd_ready, at.rstd + 1)
                    dve.scalar_tensor_tensor(x[:, m, :], x[:, m, :], sums[:, at.sum:at.sum + 1], area(A_ROWS, D),
                                             ALU.mult, ALU.mult).then_inc(x_ready, 1)
                    at.rstd += 1
                    at.sum += 1
                at.x += TT

            def cross():
                s = area(A_S, 2, S)
                normalize(memx, xn)
                turn(f"memn{at.layer['cross']}", mT_hi, mT_lo)
                normalize(x, xn)
                for j in range(2):
                    next_split()
                turn(f"crossn{at.layer['cross']}", xT_hi, xT_lo)
                for j in range(10):
                    next_split()
                u0, n = at.unit, X_HEADS * TT
                for i in range(n + 1):
                    if i < n:
                        b = nmax[:, i % 2, 0:1]
                        dve.wait_ge(logits_done, u0 + i + 1)
                        chain(dve.tensor_reduce(b, PS[:, i % 2, 0:S], AX_X, ALU.max, negate=True))
                        dve.tensor_scalar(b, b, X_DIM ** -0.5, None, ALU.mult).then_inc(max_ready, 1)
                    if i >= 1:
                        j = i - 1
                        dve.wait_ge(exp_done, u0 + j + 1)
                        chain(dve.reciprocal(rsum[:, j % 2, 0:1], esum[:, j % 2, 0:1]))
                        dve.tensor_scalar(s[:, j % 2, :], s[:, j % 2, :], rsum[:, j % 2, 0:1], None,
                                          ALU.mult).then_inc(prob_ready, 1)
                at.unit += n
                turn("ones", mT_hi, mT_lo)
                for j in range(3):
                    next_split()
                at.tile += 1
                late[0] = True
                residual(1.0)
                at.layer["cross"] += 1

            dve.memset(zeros[:], 0.0).then_inc(prep, 1)
            dve.wait_ge(setup, 64)

            def first_splits(a, b):
                for n in range(a, b):
                    split(n, n % SPL, n % RAW)
                if a == 0:
                    return
                dve.wait_ge(dtw_hi_ready, 1)
                dve.tensor_tensor(dtw_lo[:], dtw_raw, dtw_hi[:], ALU.subtract).then_inc(dtw_ready, 1)
            for stage in STAGES:
                if stage == "ffn":
                    normalize(x, xn)
                    if at.tile == 0:
                        first_splits(0, 1)
                    turn(f"ffn{at.layer['ffn']}", xT_hi, xT_lo)
                    ffn()
                    at.layer["ffn"] += 1
                elif stage == "cross":
                    cross()
                elif stage == "mixer":
                    mixer()
                elif stage == "pool":
                    pool_stage()
                elif stage == "nsa":
                    nsa()
                elif stage in ("blocknorm", "finalnorm"):
                    row_norm()


def _tiles_k1024(w):
    n = w.shape[1] // 256
    return np.ascontiguousarray(w.reshape(8, P, n, 256).transpose(2, 1, 0, 3)).reshape(n, P, 2048)


def _tiles_k256(w):
    n = w.shape[0] // 256
    return np.ascontiguousarray(w.reshape(n, 2, P, D).transpose(0, 2, 1, 3)).reshape(n, P, 2048)


def _ffn_tiles(w_in, w_out):
    g, u, o = _tiles_k1024(w_in[:, :F]), _tiles_k1024(w_in[:, F:]), _tiles_k256(w_out)
    order = [g[0], u[0]]
    for i in range(1, FI):
        order += [g[i], u[i], o[i - 1]]
    return order + [o[FI - 1]]


def _feature_cols(v):
    return v.reshape(-1, P).T


def _constants():
    con = np.zeros((P, NCONST), np.float32)
    i = np.arange(P)
    con[:, K_IDENT:K_IDENT + P] = np.eye(P)
    con[:, K_TRIU:K_TRIU + P] = i[:, None] <= i[None, :]
    con[:, K_SEGMASK:K_SEGMASK + P] = np.where(i[:, None] <= i[None, :], 0.0, NEG)
    con[:, K_CAUSAL + P:K_CAUSAL + 2 * P] = np.where(i[None, :] <= i[:, None], 0.0, NEG)
    t = np.arange(S).reshape(TT, P).T
    end = np.arange(NCMP) * CMP_STRIDE + CMP_BLOCK - 1
    vis = end[None, None, :] <= t[:, :, None]
    for m in range(TT):
        con[:, K_CMPMASK + 16 * m:K_CMPMASK + 16 * m + NCMP] = np.where(vis[:, m], 0.0, NEG)
    con[:, K_ANYVIS:K_ANYVIS + TT] = vis.any(-1)
    con[:, K_ONES:K_ONES + P] = 1.0
    con[:, K_FLIP:K_FLIP + P] = np.eye(P)[::-1]
    s, u = np.arange(S)[:, None], np.arange(S)[None, :]
    band = np.zeros((len(WINDOWS), S, S), np.float32)
    for g, w in enumerate(WINDOWS):
        inside = (s <= u) & (s > u - w)
        band[g] = inside / np.minimum(u + 1, w).astype(np.float32) - (s == u)
    band = np.ascontiguousarray(band.reshape(4, TT, P, S).transpose(2, 1, 0, 3)).reshape(P, TT * 4 * S)
    d = 255 - np.arange(384)
    n = np.maximum(d, 0)
    exact = BUCKETS // 2
    large = exact + (np.log(np.maximum(n, 1).astype(np.float32) / exact) / math.log(MAX_DIST / exact)
                     * (BUCKETS - exact)).astype(np.int32)
    bucket = np.where(n < exact, n, np.minimum(large, BUCKETS - 1))
    onehot = np.zeros((BUCKETS + 1, 384), np.float32)
    onehot[bucket, np.arange(384)] = 1.0
    onehot[BUCKETS] = np.where(d < 0, NEG, 0.0)
    return con, band, onehot


def kernel(**inp):
    from concourse import bacc
    from concourse.bass_utils import run_bass_kernel_spmd

    a = {k: np.asarray(v) for k, v in inp.items()}
    n_ffn, n_cross = 0, 0
    ffns = [(a["ffn1_w_in"][0], a["ffn1_w_out"][0]), (a["ffn2_w_in"][0], a["ffn2_w_out"][0])]
    crosses = [(a["w_ck"][0], a["w_cv"][0], a["w_cq"][0], a["w_co"][0])]
    for i in range(2):
        ffns += [(a["ffn1_w_in_2"][i], a["ffn1_w_out_2"][i]), (a["ffn2_w_in_2"][i], a["ffn2_w_out_2"][i])]
        kv = a["xattn_w_kv_2"][i]
        crosses.append((kv[:, :D], kv[:, D:], a["xattn_w_q_2"][i], a["xattn_w_o_2"][i]))
    tiles = []
    w_mix, w_nsa = a["w_in_mix"][0], a["nsa_w_in_2"][0]
    for stage in STAGES:
        if stage == "ffn":
            tiles += _ffn_tiles(*ffns[n_ffn])
            n_ffn += 1
        elif stage == "cross":
            k, v, q, o = crosses[n_cross]
            n_cross += 1
            tiles += [*_tiles_k1024(k), *_tiles_k1024(v), *_tiles_k1024(q), *_tiles_k256(o)]
        elif stage == "mixer":
            tiles += [*_tiles_k1024(w_mix[:, :3072]), *_tiles_k1024(w_mix[:, 3088:]),
                      *_tiles_k256(a["w_out_mix"][0])]
        elif stage == "pool":
            tiles += [*_tiles_k1024(a["pool_w_2"][0].reshape(D, 256))]
        elif stage == "nsa":
            w1 = a["nsa_cmp_w1_2"][0]
            tiles += [*_tiles_k1024(w_nsa[:, :1536])]
            for i in range(2):
                tiles += [_tiles_k1024(w1[i][:1024])[0], _tiles_k1024(w1[i][1024:])[0]]
            tiles += [*_tiles_k1024(w_nsa[:, 1536:2560]), *_tiles_k256(a["nsa_w_o_2"][0])]
    weights = np.stack(tiles + [np.zeros((P, 2048), np.float32)] * (SPL - 1))

    cols = np.zeros((P, NCOLS), np.float32)
    named = {"ones": np.ones(D, np.float32), "ffn0": a["norm_ffn1_w"], "mix0": a["norm_mix_w"],
             "crossn0": a["norm_cross_w"], "memn0": a["norm_mem_w"], "ffn1": a["norm_ffn2_w"],
             "ssd_norm": a["ssd_norm_w"], "subln": a["subln_w"], "conv_w": a["conv_w"],
             "conv_b": a["conv_b"], "cmp_pos": a["nsa_cmp_pos_2"]}
    for i in range(2):
        named |= {f"ffn{2 + 2 * i}": a["ffn1_norm_2"][i], f"ffn{3 + 2 * i}": a["ffn2_norm_2"][i],
                  f"mix{1 + i}": a["mix_norm_2"][i], f"crossn{1 + i}": a["xattn_norm_2"][i],
                  f"memn{1 + i}": a["mem_norm_2"][i]}
    for name, v in named.items():
        at, n = COLS[name]
        cols[:, at:at + n] = _feature_cols(v)
    con, band, onehot = _constants()
    rows = np.concatenate([a["dt_bias"][0], a["a_log"][0], a["d_skip"][0], a["lambda_q1"][0],
                           a["lambda_k1"][0], a["lambda_q2"][0], a["lambda_k2"][0]])
    rowsD = np.stack([a["norm_final_w"], a["pool_b_2"][0], a["pool_scale_2"][0], a["final_norm_2"]])
    dtw = np.concatenate([w_mix[:, 3072:3088], w_nsa[:, 2560:]], axis=1)
    dtw = np.ascontiguousarray(dtw.reshape(KC, P, 64).transpose(1, 0, 2))
    w2c = np.ascontiguousarray(a["nsa_cmp_w2_2"][0].reshape(2, 2, P, 64).transpose(2, 0, 1, 3))
    mems = np.stack([a["mem"][0], a["mem_2"][0]])

    arrays = {"weights": weights, "cols": cols, "consts": con, "rows": rows, "rowsD": rowsD, "dtw": dtw,
              "w2c": w2c, "relb": np.concatenate([a["rel_bias"], np.ones((1, DA_HEADS), np.float32)]), "onehot": onehot, "band": band,
              "x_in": a["x"][0].reshape(TT, P, D), "mems": mems.reshape(2, TT, P, D)}
    nc = bacc.Bacc("TRN2", target_bir_lowering=False, num_devices=1)
    args = [nc.dram_tensor(k, v.shape, F32, kind="ExternalInput").ap() for k, v in arrays.items()]
    out = nc.dram_tensor("out", (TT, P, D), F32, kind="ExternalOutput").ap()
    toep = nc.dram_tensor("toep", (DA_HEADS, 384), F32, kind="Internal").ap()
    program(nc, *args, out, toep)
    r = run_bass_kernel_spmd(nc, [arrays], core_ids=[0])
    return r.results[0]["out"].reshape(1, S, D)
```
